# Optimizing a Trainium2 kernel written in Bass

```python
import jax, jax.numpy as jnp
from jax import lax
import numpy as np
import math

D_MODEL = 1024
BATCH = 1
SEQ = 512
DEPTH = 1

N_MEM = 256
XATTN_HEADS = 4
XATTN_HEAD_DIM = D_MODEL // XATTN_HEADS
D_FF = 2816
GLA_HEADS = 4
GLA_DK = 64
GLA_DV = 128
GLA_KEY_W = GLA_HEADS * GLA_DK
GLA_VAL_W = GLA_HEADS * GLA_DV
GATE_RANK = 16
GATE_TAU = 16.0
CHUNK = 64
CONV_W = 512
CONV_K = 3
D_MIX = GLA_VAL_W + CONV_W
EPS = 1e-6
IN_SPLITS = (GLA_KEY_W, GLA_KEY_W, GLA_VAL_W, GLA_VAL_W, GATE_RANK, GATE_RANK,
             CONV_W, CONV_W, CONV_W)
D_IN = sum(IN_SPLITS)


def rms_norm(x, g):
    xf = x.astype(jnp.float32)
    y = xf * lax.rsqrt(jnp.mean(xf * xf, axis=-1, keepdims=True) + EPS)
    return (y * g.astype(jnp.float32)).astype(x.dtype)

def swiglu(h, w_gate, w_up, w_down):
    return (jax.nn.silu(h @ w_gate) * (h @ w_up)) @ w_down

def gla_chunked(q, k, v, g):
    b_, h_, s_, dk = q.shape
    dv = v.shape[-1]
    n = s_ // CHUNK
    q = q.reshape(b_, h_, n, CHUNK, dk)
    k = k.reshape(b_, h_, n, CHUNK, dk)
    v = v.reshape(b_, h_, n, CHUNK, dv)
    bcum = jnp.cumsum(g.reshape(b_, h_, n, CHUNK, dk), axis=3)
    b_last = bcum[:, :, :, -1:, :]
    q_in = q * jnp.exp(bcum)
    k_in = k * jnp.exp(-bcum)
    mask = jnp.tril(jnp.ones((CHUNK, CHUNK), dtype=bool))
    att = jnp.einsum('bhncd,bhnmd->bhncm', q_in, k_in)
    att = jnp.where(mask, att, 0.0)
    o_intra = jnp.einsum('bhncm,bhnmv->bhncv', att, v)
    k_st = k * jnp.exp(b_last - bcum)
    d_state = jnp.einsum('bhncd,bhncv->bhndv', k_st, v)
    decay = jnp.exp(b_last[:, :, :, 0, :])

    def step(state, inp):
        dec, ds = inp
        return dec[..., None] * state + ds, state

    init = jnp.zeros((b_, h_, dk, dv), jnp.float32)
    _, states = lax.scan(step, init, (jnp.moveaxis(decay, 2, 0), jnp.moveaxis(d_state, 2, 0)))
    states = jnp.moveaxis(states, 0, 2)
    o_inter = jnp.einsum('bhncd,bhndv->bhncv', q_in, states)
    return (o_intra + o_inter).reshape(b_, h_, s_, dv)

def low_rank_log_gate(z, w2, b2):
    zf = z.astype(jnp.float32) @ w2.astype(jnp.float32) + b2.astype(jnp.float32)
    lg = jax.nn.log_sigmoid(zf) / GATE_TAU
    bsz, s_ = z.shape[0], z.shape[1]
    return lg.reshape(bsz, s_, GLA_HEADS, GLA_DK).transpose(0, 2, 1, 3)

def to_heads(t, nh):
    bsz, s_, w = t.shape
    return t.reshape(bsz, s_, nh, w // nh).transpose(0, 2, 1, 3)

def token_mixing(h, w_in, gf_w, gf_b, gb_w, gb_b, gla_norm, conv_w, conv_b, w_out):
    bsz, s_, _ = h.shape
    proj = h @ w_in
    idx = np.cumsum(IN_SPLITS)[:-1].tolist()
    q, k, v, r, zf, zb, bg, cg, xv = jnp.split(proj, idx, axis=-1)
    qh = to_heads(q, GLA_HEADS).astype(jnp.float32) * (GLA_DK ** -0.5)
    kh = to_heads(k, GLA_HEADS).astype(jnp.float32)
    vh = to_heads(v, GLA_HEADS).astype(jnp.float32)
    g_fwd = low_rank_log_gate(zf, gf_w, gf_b)
    g_bwd = low_rank_log_gate(zb, gb_w, gb_b)
    o_fwd = gla_chunked(qh, kh, vh, g_fwd)
    flip = lambda t: jnp.flip(t, axis=2)
    o_bwd = flip(gla_chunked(flip(qh), flip(kh), flip(vh), flip(g_bwd)))
    o = o_fwd + o_bwd
    o = o * lax.rsqrt(jnp.mean(o * o, axis=-1, keepdims=True) + EPS)
    o = o * gla_norm.astype(jnp.float32).reshape(GLA_HEADS, 1, GLA_DV)
    o = o.transpose(0, 2, 1, 3).reshape(bsz, s_, GLA_VAL_W).astype(h.dtype)
    a_out = o * jax.nn.silu(r)
    u = cg * xv
    u_prev = jnp.pad(u[:, :-1], ((0, 0), (1, 0), (0, 0)))
    u_next = jnp.pad(u[:, 1:], ((0, 0), (0, 1), (0, 0)))
    conv = conv_w[0] * u_prev + conv_w[1] * u + conv_w[2] * u_next + conv_b
    c_out = bg * conv
    return jnp.concatenate([a_out, c_out], axis=-1) @ w_out

def memory_cross_attention(h, m, w_q, w_kv, w_o):
    q = to_heads(h @ w_q, XATTN_HEADS)
    kv = m @ w_kv
    k, v = jnp.split(kv, 2, axis=-1)
    k = to_heads(k, XATTN_HEADS)
    v = to_heads(v, XATTN_HEADS)
    s = jnp.einsum('bhsd,bhmd->bhsm', q.astype(jnp.float32), k.astype(jnp.float32))
    p = jax.nn.softmax(s * (XATTN_HEAD_DIM ** -0.5), axis=-1)
    o = jnp.einsum('bhsm,bhmd->bhsd', p, v.astype(jnp.float32)).astype(h.dtype)
    bsz, _, s_, _ = o.shape
    o = o.transpose(0, 2, 1, 3).reshape(bsz, s_, D_MODEL)
    return o @ w_o

def first_inputs(seed: int = 0) -> dict:
    key = jax.random.key(seed)
    ks = iter(jax.random.split(key, 40))

    def dense(shape, fan_in):
        return jax.random.normal(next(ks), shape, jnp.float32) * (fan_in ** -0.5)

    def gain(shape):
        return 1.0 + 0.02 * jax.random.normal(next(ks), shape, jnp.float32)

    def small(shape, scale=0.02, offset=0.0):
        return offset + scale * jax.random.normal(next(ks), shape, jnp.float32)

    L = DEPTH
    return {
        "x": jax.random.normal(next(ks), (BATCH, SEQ, D_MODEL), jnp.float32),
        "mem": jax.random.normal(next(ks), (BATCH, N_MEM, D_MODEL), jnp.float32),
        "ffn1_norm": gain((L, D_MODEL)),
        "ffn1_w_gate": dense((L, D_MODEL, D_FF), D_MODEL),
        "ffn1_w_up": dense((L, D_MODEL, D_FF), D_MODEL),
        "ffn1_w_down": dense((L, D_FF, D_MODEL), D_FF),
        "mix_norm": gain((L, D_MODEL)),
        "w_in": dense((L, D_MODEL, D_IN), D_MODEL),
        "gate_fwd_w": dense((L, GATE_RANK, GLA_KEY_W), GATE_RANK),
        "gate_fwd_b": small((L, GLA_KEY_W), 0.5, 1.0),
        "gate_bwd_w": dense((L, GATE_RANK, GLA_KEY_W), GATE_RANK),
        "gate_bwd_b": small((L, GLA_KEY_W), 0.5, 1.0),
        "gla_norm": gain((L, GLA_VAL_W)),
        "conv_w": dense((L, CONV_K, CONV_W), CONV_K),
        "conv_b": small((L, CONV_W)),
        "w_out": dense((L, D_MIX, D_MODEL), D_MIX),
        "xattn_norm": gain((L, D_MODEL)),
        "mem_norm": gain((L, D_MODEL)),
        "xattn_w_q": dense((L, D_MODEL, D_MODEL), D_MODEL),
        "xattn_w_kv": dense((L, D_MODEL, 2 * D_MODEL), D_MODEL),
        "xattn_w_o": dense((L, D_MODEL, D_MODEL), D_MODEL),
        "ffn2_norm": gain((L, D_MODEL)),
        "ffn2_w_gate": dense((L, D_MODEL, D_FF), D_MODEL),
        "ffn2_w_up": dense((L, D_MODEL, D_FF), D_MODEL),
        "ffn2_w_down": dense((L, D_FF, D_MODEL), D_FF),
        "final_norm": gain((D_MODEL,)),
    }

def first_block(x, mem, ffn1_norm, ffn1_w_gate, ffn1_w_up, ffn1_w_down, mix_norm, w_in,
              gate_fwd_w, gate_fwd_b, gate_bwd_w, gate_bwd_b, gla_norm, conv_w, conv_b,
              w_out, xattn_norm, mem_norm, xattn_w_q, xattn_w_kv, xattn_w_o,
              ffn2_norm, ffn2_w_gate, ffn2_w_up, ffn2_w_down, final_norm):
    for l in range(DEPTH):
        x = x + 0.5 * swiglu(rms_norm(x, ffn1_norm[l]), ffn1_w_gate[l], ffn1_w_up[l], ffn1_w_down[l])
        x = x + token_mixing(rms_norm(x, mix_norm[l]), w_in[l], gate_fwd_w[l], gate_fwd_b[l],
                             gate_bwd_w[l], gate_bwd_b[l], gla_norm[l], conv_w[l], conv_b[l], w_out[l])
        x = x + memory_cross_attention(rms_norm(x, xattn_norm[l]), rms_norm(mem, mem_norm[l]),
                                       xattn_w_q[l], xattn_w_kv[l], xattn_w_o[l])
        x = x + 0.5 * swiglu(rms_norm(x, ffn2_norm[l]), ffn2_w_gate[l], ffn2_w_up[l], ffn2_w_down[l])
    return rms_norm(x, final_norm)


DEPTH_2 = 2

Q_BLOCK = 128
ROPE_THETA = 500000.0
ROPE_FRACTION = 4
NORM_EPS = 1e-6
N_MIXERS = 2
DIFF_HEAD_DIM = 64
DIFF_HEADS = D_MODEL // (2 * DIFF_HEAD_DIM)
DIFF_V_DIM = 2 * DIFF_HEAD_DIM
DSA_HEAD_DIM = 64
DSA_HEADS = D_MODEL // DSA_HEAD_DIM
DSA_Q_RANK = D_MODEL // 4
IDX_HEADS = 8
IDX_DIM = 64
TOPK_MAX = 256
D_FF_2 = 4 * D_MODEL

N_DIFF_LAYERS = (DEPTH_2 + 1) // 2
N_DSA_LAYERS = DEPTH_2 // 2


def rms_norm_2(x, g=None):
    xf = x.astype(jnp.float32)
    y = xf * lax.rsqrt(jnp.mean(xf * xf, axis=-1, keepdims=True) + NORM_EPS)
    if g is not None:
        y = y * g.astype(jnp.float32)
    return y.astype(x.dtype)

def rope_tables(positions, head_dim):
    rot = head_dim // ROPE_FRACTION
    inv = ROPE_THETA ** (-jnp.arange(0, rot, 2, dtype=jnp.float32) / rot)
    ang = positions.astype(jnp.float32)[..., None] * inv
    return jnp.cos(ang)[:, :, None, :], jnp.sin(ang)[:, :, None, :]

def apply_partial_rope(x, cos, sin):
    half = cos.shape[-1]
    rot = 2 * half
    x1 = x[..., :half].astype(jnp.float32)
    x2 = x[..., half:rot].astype(jnp.float32)
    r = jnp.concatenate([x1 * cos - x2 * sin, x2 * cos + x1 * sin], axis=-1).astype(x.dtype)
    return jnp.concatenate([r, x[..., rot:]], axis=-1)

def diff_attention(h, w_in, q_g, k_g, lam_q1, lam_k1, lam_q2, lam_k2, subln_g, w_out,
                   cos, sin, lam_init):
    B, S, _ = h.shape
    H, d = DIFF_HEADS, DIFF_HEAD_DIM
    proj = h @ w_in
    q, k, v = jnp.split(proj, [2 * H * d, 4 * H * d], axis=-1)
    q = apply_partial_rope(rms_norm_2(q.reshape(B, S, 2 * H, d), q_g), cos, sin) * (d ** -0.5)
    k = apply_partial_rope(rms_norm_2(k.reshape(B, S, 2 * H, d), k_g), cos, sin)
    q = q.reshape(B, S, H, 2, d)
    k = k.reshape(B, S, H, 2, d)
    v = v.reshape(B, S, H, DIFF_V_DIM)
    lam = (jnp.exp(jnp.sum(lam_q1.astype(jnp.float32) * lam_k1.astype(jnp.float32)))
           - jnp.exp(jnp.sum(lam_q2.astype(jnp.float32) * lam_k2.astype(jnp.float32)))
           + lam_init)
    n_blocks = S // Q_BLOCK
    key_chunk = jnp.arange(S) // CHUNK
    q_blocks = q.reshape(B, n_blocks, Q_BLOCK, H, 2, d).swapaxes(0, 1)

    def block(args):
        qb, start = args
        q_chunk = (start + jnp.arange(Q_BLOCK)) // CHUNK
        mask = key_chunk[None, :] <= q_chunk[:, None]
        s = jnp.einsum('bqhcd,bkhcd->bhcqk', qb, k).astype(jnp.float32)
        p = jax.nn.softmax(jnp.where(mask, s, -jnp.inf), axis=-1)
        a = p[:, :, 0] - lam * p[:, :, 1]
        return jnp.einsum('bhqk,bkhe->bqhe', a.astype(v.dtype), v)

    o = lax.map(block, (q_blocks, jnp.arange(n_blocks) * Q_BLOCK))
    o = o.swapaxes(0, 1).reshape(B, S, H, DIFF_V_DIM)
    o = rms_norm_2(o, subln_g) * (1.0 - lam_init)
    return o.reshape(B, S, H * DIFF_V_DIM) @ w_out

def dsa_attention(h, w_in, cq_g, w_uq, w_uq_idx, q_g, k_g, w_out, cos, sin):
    B, S, _ = h.shape
    H, d, R, HI, DI = DSA_HEADS, DSA_HEAD_DIM, DSA_Q_RANK, IDX_HEADS, IDX_DIM
    proj = h @ w_in
    c_q, k, v, k_idx, w_idx = jnp.split(
        proj, [R, R + H * d, R + 2 * H * d, R + 2 * H * d + DI], axis=-1)
    c_q = rms_norm_2(c_q, cq_g)
    q = (c_q @ w_uq).reshape(B, S, H, d)
    q_idx = apply_partial_rope((c_q @ w_uq_idx).reshape(B, S, HI, DI), cos, sin)
    k_idx = apply_partial_rope(rms_norm_2(k_idx)[:, :, None, :], cos, sin)[:, :, 0]
    w_idx = w_idx * ((HI ** -0.5) * (DI ** -0.5))
    q = apply_partial_rope(rms_norm_2(q, q_g), cos, sin) * (d ** -0.5)
    k = apply_partial_rope(rms_norm_2(k.reshape(B, S, H, d), k_g), cos, sin)
    v = v.reshape(B, S, H, d)
    topk = min(TOPK_MAX, S // 4)
    n_blocks = S // Q_BLOCK
    key_chunk = jnp.arange(S) // CHUNK
    qb_all = q.reshape(B, n_blocks, Q_BLOCK, H, d).swapaxes(0, 1)
    qib_all = q_idx.reshape(B, n_blocks, Q_BLOCK, HI, DI).swapaxes(0, 1)
    wb_all = w_idx.reshape(B, n_blocks, Q_BLOCK, HI).swapaxes(0, 1)
    gather = jax.vmap(lambda arr, ids: arr[ids])

    def block(args):
        qb, qib, wb, start = args
        q_chunk = (start + jnp.arange(Q_BLOCK)) // CHUNK
        mask = key_chunk[None, :] <= q_chunk[:, None]
        dots = jnp.einsum('bqhe,bke->bqhk', qib, k_idx).astype(jnp.float32)
        score = jnp.einsum('bqh,bqhk->bqk', wb.astype(jnp.float32), jax.nn.relu(dots))
        score = jnp.where(mask, score, -jnp.inf)
        vals, idx = lax.top_k(score, topk)
        valid = jnp.isfinite(vals)
        kg = gather(k, idx)
        vg = gather(v, idx)
        s = jnp.einsum('bqhd,bqkhd->bhqk', qb, kg).astype(jnp.float32)
        p = jax.nn.softmax(jnp.where(valid[:, None], s, -jnp.inf), axis=-1)
        return jnp.einsum('bhqk,bqkhd->bqhd', p.astype(vg.dtype), vg)

    o = lax.map(block, (qb_all, qib_all, wb_all, jnp.arange(n_blocks) * Q_BLOCK))
    o = o.swapaxes(0, 1).reshape(B, S, H * d)
    return o @ w_out

def sq_relu_mlp(h, w1, w2):
    u = jax.nn.relu(h @ w1)
    return (u * u) @ w2

def second_inputs(seed: int = 0) -> dict:
    key = jax.random.key(seed)
    ks = iter(jax.random.split(key, 32))
    D = D_MODEL

    def nrm(shape, scale):
        return jax.random.normal(next(ks), shape, jnp.float32) * scale

    def gain(shape):
        return 1.0 + nrm(shape, 0.02)

    nA, nB = N_DIFF_LAYERS, N_DSA_LAYERS
    dsa_in = DSA_Q_RANK + 2 * DSA_HEADS * DSA_HEAD_DIM + IDX_DIM + IDX_HEADS
    x = nrm((BATCH, SEQ, D), 1.0)
    offset = jax.random.randint(next(ks), (BATCH, 1), 0, 4096, dtype=jnp.int32)
    positions = (offset + jnp.arange(SEQ, dtype=jnp.int32)[None, :]).astype(jnp.int32)
    return {
        "x": x,
        "positions": positions,
        "norm_mix": gain((DEPTH_2, D)),
        "norm_mlp": gain((DEPTH_2, D)),
        "mlp_w1": nrm((DEPTH_2, D, D_FF_2), D ** -0.5),
        "mlp_w2": nrm((DEPTH_2, D_FF_2, D), D_FF_2 ** -0.5),
        "diff_w_in": nrm((nA, D, 6 * DIFF_HEADS * DIFF_HEAD_DIM), D ** -0.5),
        "diff_q_norm": gain((nA, DIFF_HEAD_DIM)),
        "diff_k_norm": gain((nA, DIFF_HEAD_DIM)),
        "diff_lam_q1": nrm((nA, DIFF_HEAD_DIM), 0.1),
        "diff_lam_k1": nrm((nA, DIFF_HEAD_DIM), 0.1),
        "diff_lam_q2": nrm((nA, DIFF_HEAD_DIM), 0.1),
        "diff_lam_k2": nrm((nA, DIFF_HEAD_DIM), 0.1),
        "diff_subln": gain((nA, DIFF_V_DIM)),
        "diff_w_out": nrm((nA, DIFF_HEADS * DIFF_V_DIM, D), (DIFF_HEADS * DIFF_V_DIM) ** -0.5),
        "dsa_w_in": nrm((nB, D, dsa_in), D ** -0.5),
        "dsa_cq_norm": gain((nB, DSA_Q_RANK)),
        "dsa_w_uq": nrm((nB, DSA_Q_RANK, DSA_HEADS * DSA_HEAD_DIM), DSA_Q_RANK ** -0.5),
        "dsa_w_uq_idx": nrm((nB, DSA_Q_RANK, IDX_HEADS * IDX_DIM), DSA_Q_RANK ** -0.5),
        "dsa_q_norm": gain((nB, DSA_HEAD_DIM)),
        "dsa_k_norm": gain((nB, DSA_HEAD_DIM)),
        "dsa_w_out": nrm((nB, DSA_HEADS * DSA_HEAD_DIM, D), (DSA_HEADS * DSA_HEAD_DIM) ** -0.5),
    }

def second_block(x, positions, norm_mix, norm_mlp, mlp_w1, mlp_w2,
              diff_w_in, diff_q_norm, diff_k_norm, diff_lam_q1, diff_lam_k1,
              diff_lam_q2, diff_lam_k2, diff_subln, diff_w_out,
              dsa_w_in, dsa_cq_norm, dsa_w_uq, dsa_w_uq_idx, dsa_q_norm, dsa_k_norm,
              dsa_w_out):
    cos, sin = rope_tables(positions, DIFF_HEAD_DIM)
    for i in range(DEPTH_2):
        h = rms_norm_2(x, norm_mix[i])
        j = i // N_MIXERS
        if i % N_MIXERS == 0:
            lam_init = 0.8 - 0.6 * math.exp(-0.3 * i)
            mix = diff_attention(h, diff_w_in[j], diff_q_norm[j], diff_k_norm[j],
                                 diff_lam_q1[j], diff_lam_k1[j], diff_lam_q2[j],
                                 diff_lam_k2[j], diff_subln[j], diff_w_out[j],
                                 cos, sin, lam_init)
        else:
            mix = dsa_attention(h, dsa_w_in[j], dsa_cq_norm[j], dsa_w_uq[j],
                                dsa_w_uq_idx[j], dsa_q_norm[j], dsa_k_norm[j],
                                dsa_w_out[j], cos, sin)
        x = x + mix
        x = x + sq_relu_mlp(rms_norm_2(x, norm_mlp[i]), mlp_w1[i], mlp_w2[i])
    return x


def setup_inputs(seed=0):
    out = dict(first_inputs(seed))
    for name, value in second_inputs(seed + 1).items():
        if name != "x":
            out[name + "_2"] = value
    return out


def reference(
    x, mem, ffn1_norm, ffn1_w_gate, ffn1_w_up, ffn1_w_down, mix_norm, w_in, gate_fwd_w,
    gate_fwd_b, gate_bwd_w, gate_bwd_b, gla_norm, conv_w, conv_b, w_out, xattn_norm, mem_norm,
    xattn_w_q, xattn_w_kv, xattn_w_o, ffn2_norm, ffn2_w_gate, ffn2_w_up, ffn2_w_down,
    final_norm, positions_2, norm_mix_2, norm_mlp_2, mlp_w1_2, mlp_w2_2, diff_w_in_2,
    diff_q_norm_2, diff_k_norm_2, diff_lam_q1_2, diff_lam_k1_2, diff_lam_q2_2, diff_lam_k2_2,
    diff_subln_2, diff_w_out_2, dsa_w_in_2, dsa_cq_norm_2, dsa_w_uq_2, dsa_w_uq_idx_2,
    dsa_q_norm_2, dsa_k_norm_2, dsa_w_out_2,
):
    x = first_block(
        x, mem, ffn1_norm, ffn1_w_gate, ffn1_w_up, ffn1_w_down, mix_norm, w_in, gate_fwd_w,
        gate_fwd_b, gate_bwd_w, gate_bwd_b, gla_norm, conv_w, conv_b, w_out, xattn_norm,
        mem_norm, xattn_w_q, xattn_w_kv, xattn_w_o, ffn2_norm, ffn2_w_gate, ffn2_w_up,
        ffn2_w_down, final_norm,
    )
    return second_block(
        x, positions_2, norm_mix_2, norm_mlp_2, mlp_w1_2, mlp_w2_2, diff_w_in_2, diff_q_norm_2,
        diff_k_norm_2, diff_lam_q1_2, diff_lam_k1_2, diff_lam_q2_2, diff_lam_k2_2, diff_subln_2,
        diff_w_out_2, dsa_w_in_2, dsa_cq_norm_2, dsa_w_uq_2, dsa_w_uq_idx_2, dsa_q_norm_2,
        dsa_k_norm_2, dsa_w_out_2,
    )


_drawn_inputs = setup_inputs


def setup_inputs(seed=0):
    import zlib

    import numpy as np

    out = dict(_drawn_inputs(seed))
    spreads = {}
    factors = {'ffn1_norm': 3.234,
     'gla_norm': 5.326,
     'conv_b': 3.649,
     'xattn_norm': 8.0,
     'mem_norm': 6.105,
     'ffn2_norm': 5.36,
     'diff_q_norm_2': 4.326,
     'diff_k_norm_2': 4.337,
     'diff_lam_k1_2': 5.726,
     'diff_subln_2': 3.516,
     'dsa_cq_norm_2': 7.414,
     'dsa_q_norm_2': 8.0,
     'dsa_k_norm_2': 8.0}
    for name, (base, spread) in spreads.items():
        noise = np.random.default_rng([zlib.crc32(name.encode()), seed]).standard_normal(out[name].shape)
        drawn = base * np.exp(spread * noise) if base else spread * noise
        out[name] = __import__('jax').numpy.asarray(drawn.astype(out[name].dtype))
    for name, factor in factors.items():
        out[name] = (out[name] * factor).astype(out[name].dtype)
    return out
```

```python
from contextlib import ExitStack

import numpy as np

import concourse.bass as bass
from concourse import mybir

F32 = mybir.dt.float32
F32R = mybir.dt.float32r
I32 = mybir.dt.int32
ACT = mybir.ActivationFunctionType
ALU = mybir.AluOpType
AX_X = mybir.AxisListType.X
ts, ds = bass.ts, bass.ds

P = 128
S = 512
D = 1024
KT = D // P
ST = S // P
NMEM = 256
MT = NMEM // P
BLK = 16 * P
FF1, FF2 = 2816, 4096
EPS = 1e-6
NEG = -1.0e30
GONE = -3.0e38
LN_SET, SILU_SET = "natural_log_exp_and_others", "silu_and_others"

GH, GDK, GDV, CH = 4, 64, 128, 64
NCH = S // CH
Q0, K0, V0, R0, Z0, BG0, CG0, XV0 = 0, 256, 512, 1024, 1536, 1568, 2080, 2592
ZW = 32

SH, IH, TOPK = 16, 8, 128
ROT = 8
ROPE_INV = [float(np.float32(500000.0) ** np.float32(-i / ROT)) for i in range(ROT)]
_two_pi, TWO_PI = 2 * np.pi, []
for _step in (2.0 ** -5, 2.0 ** -14, 2.0 ** -23, 2.0 ** -32, 2.0 ** -41):
    TWO_PI.append(float(np.floor(_two_pi / _step) * _step))
    _two_pi -= TWO_PI[-1]

PARAM_ROWS = dict(ffn1_norm=8, mix_norm=8, xattn_norm=8, mem_norm=8, ffn2_norm=8, final_norm=8,
                  norm_mix_2=16, norm_mlp_2=16, gate_fwd_b=2, gate_bwd_b=2, gla_norm=4,
                  conv_w=12, conv_b=4)
PARAM_AT, _n = {}, 0
for _k, _v in PARAM_ROWS.items():
    PARAM_AT[_k] = _n
    _n += _v
NPARAM = _n
ROWP = dict(diff_q_norm_2=64, diff_k_norm_2=64, diff_subln_2=128, dsa_cq_norm_2=256,
            dsa_q_norm_2=64, dsa_k_norm_2=64, diff_lam_q1_2=64, diff_lam_k1_2=64,
            diff_lam_q2_2=64, diff_lam_k2_2=64)
ROWP_AT, _n = {}, 0
for _k, _v in ROWP.items():
    ROWP_AT[_k] = _n
    _n += _v
NROWP = _n


class Pass:

    def __init__(self, name, swiglu, tiles, scale, norm, half=0):
        self.name, self.swiglu, self.tiles, self.scale = name, swiglu, tiles, scale
        self.norm, self.half = norm, half
        self.up_blocks = tiles if swiglu else tiles // 2
        self.down_blocks = tiles // 2
        self.iters = self.up_blocks // 2
        self.step = 2 if swiglu else 4


SWIGLU1 = Pass("ffn1", True, FF1 // P, 0.5, 0)
SWIGLU2 = Pass("ffn2", True, FF1 // P, 0.5, 3)
MLP = [Pass("mlp", False, FF2 // P // 2, 1.0, 5 + 2 * (i // 2), i) for i in range(4)]
N_FFN1, N_MIX, N_X, N_FFN2, N_FINAL, N_DIFF, N_MLP0, N_DSA, N_MLP1 = range(9)
SWIGLU2.norm = N_FFN2
for _i, _p in enumerate(MLP):
    _p.norm = N_MLP0 if _i < 2 else N_MLP1
MIX_BLOCKS, X_BLOCKS, DIFF_BLOCKS, DSA_BLOCKS, OUT_BLOCKS = 13, 12, 12, 12, 4


def plan(stop):
    at, b, tile, upd, down = {}, 0, 0, 1, 0
    stages = [SWIGLU1, ("mix", MIX_BLOCKS), ("x", X_BLOCKS), SWIGLU2, "final", ("diff", DIFF_BLOCKS),
              MLP[0], MLP[1], ("dsa", DSA_BLOCKS), MLP[2], MLP[3]]
    for n, st in enumerate(stages[:stop]):
        if isinstance(st, Pass):
            st.b, st.tile, st.upd, st.down = b, tile, upd, down
            b += st.up_blocks + st.down_blocks
            tile += st.tiles
            upd, down = upd + 1, down + KT - 1
        elif st == "final":
            at[st] = (b, upd, down)
            upd += 1
        else:
            at[st[0]] = (b, upd, down)
            b += st[1] + OUT_BLOCKS
            upd, down = upd + 1, down + KT // 2
    return stages[:stop], at, b, upd


def hn(n):
    return n - (n > N_FINAL)


def wait(eng, sem, value):
    if not isinstance(value, int) or value > 0:
        eng.wait_ge(sem, value)


LAM_INIT = 0.8 - 0.6
NVC = 5


def row_banks(diff_b, dsa_b):
    ends = [(diff_b + 2 * g + 1, True) for g in range(6)]
    ends += [(dsa_b + j, last) for j, last in ((0, 1), (1, 1), (3, 1), (4, 1), (5, 0), (5, 1), (7, 1),
                                               (9, 1), (11, 1))]
    banks, n = [], 0
    for b, last in ends:
        for st in range(ST):
            if st == ST - 1 and last:
                banks.append(("block", b + 1))
            else:
                n += 1
                banks.append(("bank", n))
    return banks


class Chain:

    def __init__(self, eng, sem):
        self.eng, self.sem, self.n, self.loop = eng, sem, 0, 0

    def done(self, ins):
        ins.then_inc(self.sem, 1)
        self.n += 1

    def link(self, ins):
        self.done(ins)
        self.eng.wait_ge(self.sem, self.loop + self.n)

    def wait(self):
        self.eng.wait_ge(self.sem, self.loop + self.n)

    def enter(self, i, per):
        self.loop, self.per, self.start = i * per, per, self.n

    def leave(self, rounds):
        assert self.n - self.start == self.per, (self.n, self.start, self.per)
        self.loop, self.n = 0, self.start + self.per * rounds


def two_blocks(nc, dram, out, stop=11):
    stages, at, nblocks, nupd = plan(stop)
    bank_ends = row_banks(at["diff"][0] if "diff" in at else 0, at["dsa"][0] if "dsa" in at else 0)
    K = 1024
    XT, HH, HL, ARENA, RAW, WHI, WLO = 0, 16 * K, 32 * K, 48 * K, 136 * K, 152 * K, 168 * K
    SG, SQ, RSTD, T1, CONST = 184 * K, 192 * K, 196 * K, 198 * K, 202 * K

    ctx = ExitStack()
    with ctx:
        def put(name, shape, offset, dt=F32):
            return nc.alloc_sbuf_tensor_at(name, shape, dt, offset=offset + 2 * K)

        def arena(name, shape, kb, dt=F32):
            return put(name, shape, ARENA + kb * K, dt)

        def sem(name):
            return ctx.enter_context(nc.semaphore(name))

        const_at = [CONST]

        def const(name, shape, dt=F32):
            t = put(name, shape, const_at[0], dt)
            n = 4 * int(np.prod(shape[1:]))
            const_at[0] += (n + 31) // 32 * 32
            assert const_at[0] + 2 * K <= nc.sbuf_usable_end
            return t

        xT = put("xT", [P, KT, S], XT)
        hh = put("hh", [P, KT, S], HH, F32R)
        hl = put("hl", [P, KT, S], HL, F32R)
        raw = put("raw", [P, 2, BLK], RAW)
        whi = put("whi", [P, 2, BLK], WHI, F32R)
        wlo = put("wlo", [P, 2, BLK], WLO, F32R)
        sg = put("sg", [P, 4, S], SG)
        sq = put("sq", [P, 2, S], SQ)
        rstd = put("rstd", [P, S], RSTD)
        t1 = put("t1", [P, 2, S], T1)
        ident = const("ident", [P, P])
        ones = const("ones", [P, P])
        params = const("params", [P, NPARAM])
        rowp = const("rowp", [P, NROWP])
        gate_w = const("gate_w", [ZW, 2, GH * GDK])
        cap = const("cap", [P, 2, P])
        ncap = const("ncap", [P, 2, P])
        carry = const("carry", [P, S])
        cosr = const("cosr", [P, ST, ROT])
        sinr = const("sinr", [P, ST, ROT])
        rt = const("rt", [P, 4, ST, ROT])
        posi = const("posi", [P, ST], I32)
        one = const("one", [P, 1])
        halfpi = const("halfpi", [P, 1])
        lam = const("lam", [P, 4])
        lam_tmp = const("lam_tmp", [P, 64])
        small = const("small", [P, 64])
        newton = const("newton", [P, 2, 32])
        c_rs = const("c_rs", [P, 64])
        c_best = const("c_best", [P, 8])
        gh = arena("gh", [P, 22, S], 0, F32R)
        gl = arena("gl", [P, 22, S], 44, F32R)
        xrows = arena("xrows", [P, ST, D], 0)
        prow = arena("prow", [NPARAM, P], 16)
        orows = arena("orows", [P, ST, D], 0)
        m_qT = arena("m_qT", [P, 2, S], 0)
        m_kT = arena("m_kT", [P, 2, S], 4)
        m_kst_row = arena("m_kst_row", [P, 2, 2, ST, P], 0)
        m_half = arena("m_half", [P, 4, S], 0)
        m_v = arena("m_v", [P, ST, S], 8)
        m_r = arena("m_r", [P, 4, S], 16)
        m_u = arena("m_u", [P, 4, S], 24)
        m_g = arena("m_g", [P, 2, 2, S], 32)
        m_b = arena("m_b", [P, 2, 2, S], 40)
        m_state = arena("m_state", [P, 2, 2, NCH, GDV], 32)
        m_qin = arena("m_qin", [P, 2, 2, S], 48)
        m_kin = arena("m_kin", [P, 2, 2, S], 56)
        m_kst = arena("m_kst", [P, 2, 2, S], 64)
        m_tmp = arena("m_tmp", [P, 2, 2, S], 72)
        m_att = arena("m_att", [P, 4, S], 72)
        m_o = arena("m_o", [P, 4, S], 80)
        m_conv = arena("m_conv", [P, 4, S], 64)
        m_hi = arena("m_hi", [P, KT, S], 32, F32R)
        m_lo = arena("m_lo", [P, KT, S], 48, F32R)
        m_z = put("m_z", [P, S], SG)
        m_dech = put("m_dech", [P, 2, 2, NCH], SG + 2 * K)
        m_dec = put("m_dec", [P, 2, 2, NCH], SG + 3 * K)
        m_rstd = put("m_rstd", [P, 4, S], SG)
        x_mrow = arena("x_mrow", [P, MT, D], 0)
        x_memT = arena("x_memT", [P, KT, NMEM], 8)
        x_mh = arena("x_mh", [P, KT, NMEM], 16, F32R)
        x_ml = arena("x_ml", [P, KT, NMEM], 24, F32R)
        x_kT = arena("x_kT", [P, KT, NMEM], 32)
        x_v = arena("x_v", [P, MT, D], 40)
        x_qT = arena("x_qT", [P, KT, S], 48)
        x_p = arena("x_p", [P, 2, ST, NMEM], 64)
        x_pT = arena("x_pT", [P, 2, MT, S], 72)
        a_v = arena("a_v", [P, ST, D], 0)
        a_qT = arena("a_qT", [P, KT, S], 16)
        a_kT = arena("a_kT", [P, KT, S], 32)
        a_rows = arena("a_rows", [P, 2, ST, S], 48)
        a_sq = arena("a_sq", [P, ST, S], 64)
        d_p = arena("d_p", [P, 2, 2, S], 48)
        d_a = arena("d_a", [P, 2, S], 56)
        d_aT = arena("d_aT", [P, 2, S], 60)
        d_o = arena("d_o", [P, 2, S], 64)
        d_osq = arena("d_osq", [P, S], 68)
        c_bias = arena("c_bias", [P, 1280], 72)
        c_score = arena("c_score", [P, 1280], 77)
        c_work = arena("c_work", [P, 1280], 82)
        c_cq = arena("c_cq", [P, ST, 256], 0)
        c_kid = arena("c_kid", [P, ST, P], 4)
        c_cqh = arena("c_cqh", [P, 2, S], 40, F32R)
        c_cql = arena("c_cql", [P, 2, S], 44, F32R)
        c_qiT = arena("c_qiT", [P, 4, S], 16)
        c_kiT = arena("c_kiT", [P, S], 24)
        c_relu = arena("c_relu", [P, 2, S], 26)
        c_s = arena("c_s", [P, 4, S], 64)
        c_p = arena("c_p", [P, 2, S], 52)
        c_pT = arena("c_pT", [P, 2, S], 56)
        c_o = arena("c_o", [P, 2, S], 60)

        ps = ctx.enter_context(nc.psum_tensor("ps", [P, 8, S], F32))

        s_in = sem("s_in")
        s_raw = [sem("s_raw0"), sem("s_raw1")]
        s_hi = sem("s_hi")
        s_lo = sem("s_lo")
        s_used = sem("s_used")
        s_const = sem("s_const")
        s_vconst = sem("s_vconst")
        s_tr0 = sem("s_tr0")
        s_par = sem("s_par")
        s_x = sem("s_x")
        s_sq = sem("s_sq")
        s_ss = sem("s_ss")
        s_half = sem("s_half")
        s_mvar = sem("s_mvar")
        s_xmvar = sem("s_xmvar")
        s_rvar = sem("s_rvar")
        s_dovar = sem("s_dovar")
        s_rstd = sem("s_rstd")
        s_t1 = sem("s_t1")
        s_hh = sem("s_hh")
        s_hl = sem("s_hl")
        s_sg = sem("s_sg")
        s_g = sem("s_g")
        s_down = sem("s_down")
        s_ac = sem("s_ac")
        s_dv = sem("s_dv")
        s_ot = sem("s_ot")
        s_orow = sem("s_orow")
        s_out = sem("s_out")

        s_lam = sem("s_lam")
        s_lam2 = sem("s_lam2")
        s_in2 = sem("s_in2")
        s_pl = sem("s_pl")
        s_orow_v = sem("s_orow_v")
        s_memrow = sem("s_memrow")
        s_ang = sem("s_ang")
        s_rope = sem("s_rope")
        s_mz = sem("s_mz")
        s_mgate = sem("s_mgate")
        s_mzg = sem("s_mzg")
        s_mlog = sem("s_mlog")
        s_mscan = sem("s_mscan")
        s_mhalf = sem("s_mhalf")
        s_mexp = sem("s_mexp")
        s_mqk = sem("s_mqk")
        s_mv = sem("s_mv")
        s_mr = sem("s_mr")
        s_mc = sem("s_mc")
        s_mkin = sem("s_mkin")
        s_mkt = sem("s_mkt")
        s_mktc = sem("s_mktc")
        s_mds = sem("s_mds")
        s_mst = sem("s_mst")
        s_matt = sem("s_matt")
        s_matc = sem("s_matc")
        s_mot = sem("s_mot")
        s_mo = sem("s_mo")
        s_mosq = sem("s_mosq")
        s_mss = sem("s_mss")
        s_mrstd = sem("s_mrstd")
        s_mu = sem("s_mu")
        s_mn = sem("s_mn")
        s_mhi = sem("s_mhi")
        s_mfin = sem("s_mfin")
        s_xmT = sem("s_xmT")
        s_xm = sem("s_xm")
        s_xmsq = sem("s_xmsq")
        s_xmss = sem("s_xmss")
        s_xmrstd = sem("s_xmrstd")
        s_xmt1 = sem("s_xmt1")
        s_xmh = sem("s_xmh")
        s_xml = sem("s_xml")
        s_xk = sem("s_xk")
        s_xv = sem("s_xv")
        s_xq = sem("s_xq")
        s_xs = sem("s_xs")
        s_xmax = sem("s_xmax")
        s_xe = sem("s_xe")
        s_xn = sem("s_xn")
        s_xT = sem("s_xT")
        s_xpT = sem("s_xpT")
        s_xo = sem("s_xo")
        s_xol = sem("s_xol")
        s_rb = sem("s_rb")
        s_rcopy = sem("s_rcopy")
        s_rss = sem("s_rss")
        s_rrs = sem("s_rrs")
        s_rows = sem("s_rows")
        s_rt = sem("s_rt")
        s_rtc = sem("s_rtc")
        s_rss2 = sem("s_rss2")
        s_rrs2 = sem("s_rrs2")
        s_ds = sem("s_ds")
        s_dmax = sem("s_dmax")
        s_de = sem("s_de")
        s_da = sem("s_da")
        s_dT = sem("s_dT")
        s_daT = sem("s_daT")
        s_dpv = sem("s_dpv")
        s_dor = sem("s_dor")
        s_dosq = sem("s_dosq")
        s_doss = sem("s_doss")
        s_dors = sem("s_dors")
        s_don = sem("s_don")
        s_doT = sem("s_doT")
        s_dhl = sem("s_dhl")
        s_ccq = sem("s_ccq")
        s_ccqr = sem("s_ccqr")
        s_ccqn = sem("s_ccqn")
        s_cqT = sem("s_cqT")
        s_cqh = sem("s_cqh")
        s_cql = sem("s_cql")
        s_cid = sem("s_cid")
        s_cidr = sem("s_cidr")
        s_cidn = sem("s_cidn")
        s_ckT = sem("s_ckT")
        s_ckTc = sem("s_ckTc")
        s_cdot = sem("s_cdot")
        s_crelu = sem("s_crelu")
        s_cacc = sem("s_cacc")
        s_cs0 = sem("s_cs0")
        s_cs = sem("s_cs")
        s_ce = sem("s_ce")
        s_cT = sem("s_cT")
        s_cpTa = sem("s_cpTa")
        s_cpTd = sem("s_cpTd")
        s_cpv = sem("s_cpv")
        s_cor = sem("s_cor")
        s_coT = sem("s_coT")
        s_chl = sem("s_chl")

        def col(name, i):
            return params[:, PARAM_AT[name] + i:PARAM_AT[name] + i + 1]

        def row(name):
            return rowp[:, ROWP_AT[name]:ROWP_AT[name] + ROWP[name]]

        def row_bank_ready(k):
            what, n = bank_ends[k]
            return (s_used if what == "block" else s_rb), n

        NORM_GAIN = {N_FFN1: ("ffn1_norm", 0), N_MIX: ("mix_norm", 0), N_X: ("xattn_norm", 0),
                     N_FFN2: ("ffn2_norm", 0), N_FINAL: ("final_norm", 0),
                     N_DIFF: ("norm_mix_2", 0), N_MLP0: ("norm_mlp_2", 0),
                     N_DSA: ("norm_mix_2", 8), N_MLP1: ("norm_mlp_2", 8)}

        def cols_of(w, width=256):
            return w.rearrange("(k p) n -> p k n", p=P)

        def up_src(w, c0=0):
            v = cols_of(w)
            return lambda i: v[:, :, ds(c0 + i * 256, 256)]

        def down_src(w, k0=0):
            v = cols_of(w)
            return lambda i: v[:, ds(k0 + i * 2, 2), :]

        def wide_src(w, c0):
            v = cols_of(w)
            return lambda i: v[:, 4 * i:4 * i + 4, c0:c0 + 512]

        wdram = {n: dram[n][0] for n in (
            "ffn1_w_gate", "ffn1_w_up", "ffn1_w_down", "w_in", "w_out", "xattn_w_q", "xattn_w_kv",
            "xattn_w_o", "ffn2_w_gate", "ffn2_w_up", "ffn2_w_down", "diff_w_in_2", "diff_w_out_2",
            "dsa_w_in_2", "dsa_w_uq_2", "dsa_w_uq_idx_2", "dsa_w_out_2")}

        block = ctx.enter_context(nc.Block())

        @block.sync
        def _(sp):
            def load(b, src):
                n = int(np.prod(src.shape[1:]))
                dst = raw[:, b % 2, 0:n].rearrange("p (k n) -> p k n", n=src.shape[-1])
                sp.dma_start(dst, src).then_inc(s_raw[b % 2], 16)

            def stream(b0, srcs, rounds):
                m = len(srcs)
                if rounds >= 3:
                    with sp.Fori(0, rounds) as i:
                        for j in range(m):
                            sp.wait_ge(s_lo, i * m + (b0 + j - 1))
                            load(b0 + j, srcs[j](i))
                else:
                    for i in range(rounds):
                        for j in range(m):
                            b = b0 + i * m + j
                            if b >= 2:
                                sp.wait_ge(s_lo, b - 1)
                            load(b, srcs[j](i))
                return b0 + m * rounds

            def pairs(src):
                return [lambda i: src(2 * i), lambda i: src(2 * i + 1)]

            sp.dma_start(xrows[:, :, :], dram["x"][0].rearrange("(t p) d -> p t d", p=P)).then_inc(s_in, 16)
            b = 0
            for stage in stages:
                if isinstance(stage, Pass):
                    if stage.swiglu:
                        g, u = wdram[stage.name + "_w_gate"], wdram[stage.name + "_w_up"]
                        if b == 0:
                            load(0, up_src(g)(0))
                            load(1, up_src(u)(0))
                            b = stream(2, [up_src(g, 256), up_src(u, 256)], stage.iters - 1)
                        else:
                            b = stream(b, [up_src(g), up_src(u)], stage.iters)
                        down, k0 = wdram[stage.name + "_w_down"], 0
                    else:
                        layer, part = stage.half // 2, stage.half % 2
                        up = dram["mlp_w1_2"][layer]
                        b = stream(b, pairs(up_src(up, part * FF2 // 2)), stage.iters)
                        down, k0 = dram["mlp_w2_2"][layer], part * stage.tiles
                    n = stage.down_blocks
                    b = stream(b, pairs(down_src(down, k0)), n // 2)
                    if n % 2:
                        b = stream(b, [lambda i: down_src(down, k0)(n - 1)], 1)
                elif stage == "final":
                    pass
                elif stage[0] == "mix":
                    w = wdram["w_in"]
                    b = stream(b, [up_src(w, Z0)], 1)
                    b = stream(b, [up_src(w, Q0), up_src(w, K0)], 1)
                    b = stream(b, [wide_src(w, V0)], 2)
                    for c0 in (R0, CG0, XV0, BG0):
                        b = stream(b, [up_src(w, c0)], 2)
                    b = stream(b, pairs(up_src(wdram["w_out"])), 2)
                elif stage[0] == "x":
                    sp.wait_ge(s_x, 8 * at["x"][1])
                    sp.dma_start(x_mrow[:, :, :], dram["mem"][0].rearrange("(t p) d -> p t d", p=P))\
                        .then_inc(s_memrow, 16)
                    b = stream(b, pairs(up_src(wdram["xattn_w_kv"])), 2)
                    for g in range(2):
                        b = stream(b, [wide_src(wdram["xattn_w_kv"], D + 512 * g)], 2)
                    b = stream(b, pairs(up_src(wdram["xattn_w_q"])), 2)
                    b = stream(b, pairs(up_src(wdram["xattn_w_o"])), 2)
                elif stage[0] == "diff":
                    for g in range(6):
                        b = stream(b, [wide_src(wdram["diff_w_in_2"], 512 * g)], 2)
                    b = stream(b, pairs(up_src(wdram["diff_w_out_2"])), 2)
                else:
                    w = wdram["dsa_w_in_2"]
                    b = stream(b, [up_src(w, 0), up_src(w, 2120)], 1)
                    b = stream(b, [wide_src(w, 256)], 2)
                    b = stream(b, [lambda i: cols_of(wdram["dsa_w_uq_idx_2"])], 1)
                    b = stream(b, [lambda i: cols_of(wdram["dsa_w_uq_2"])], 1)
                    for c0 in (768, 1280, 1792):
                        b = stream(b, [wide_src(w, c0)], 2)
                    b = stream(b, pairs(up_src(wdram["dsa_w_out_2"])), 2)
            assert b == nblocks
            o_v = out[0].rearrange("(t p) d -> p t d", p=P)
            for st in range(ST):
                sp.wait_ge(s_orow, st + 1)
                sp.wait_ge(s_orow_v, st + 1)
                sp.dma_start(o_v[:, st, :], orows[:, st, :]).then_inc(s_out, 16)
            sp.wait_ge(s_out, 16 * ST)

        @block.gpsimd
        def _(pool):
            nc.gpsimd.memset(ident[:, :], 0.0).then_inc(s_pl, 1)
            nc.gpsimd.memset(ones[:, :], 1.0).then_inc(s_pl, 1)
            nc.gpsimd.memset(carry[:, :], 1.0).then_inc(s_pl, 1)
            nc.gpsimd.memset(cap[:, :, :], 3.0e38).then_inc(s_pl, 1)
            nc.gpsimd.memset(ncap[:, :, :], -3.0e38).then_inc(s_pl, 1)
            pool.wait_ge(s_pl, 5)
            nc.gpsimd.affine_select(out=ident[:, :], in_=ident[:, :], compare_op=ALU.not_equal, fill=1.0,
                                    base=0, pattern=[[-1, P]], channel_multiplier=1).then_inc(s_const, 1)
            for m in (cap, ncap):
                nc.gpsimd.affine_select(out=m[:, 0, :], in_=m[:, 0, :], compare_op=ALU.is_ge, fill=0.0,
                                        base=0, pattern=[[1, P]], channel_multiplier=-1).then_inc(s_pl, 1)
                nc.gpsimd.affine_select(out=m[:, 1, :], in_=m[:, 1, :], compare_op=ALU.is_ge, fill=0.0,
                                        base=0, pattern=[[-1, P]], channel_multiplier=1).then_inc(s_pl, 1)
            pool.wait_ge(s_pl, 9)
            for n, m in enumerate((cap, ncap)):
                pool.wait_ge(s_const, 2 * n + 1)
                nc.gpsimd.memset(m[0:CH, :, CH:P], 0.0).then_inc(s_const, 1)
                pool.wait_ge(s_const, 2 * n + 2)
                nc.gpsimd.memset(m[CH:P, :, 0:CH], 0.0).then_inc(s_const, 1)
            pool.wait_ge(s_const, 5)
            nc.gpsimd.memset(carry[:, 0:S:CH], 0.0).then_inc(s_const, 1)

            def split(b, in_loop=None):
                if in_loop is None:
                    pool.wait_ge(s_hi, b + 1)
                    if b >= 2:
                        pool.wait_ge(s_used, b - 1)
                else:
                    pool.wait_ge(s_hi, in_loop * 2 + (b + 1))
                    pool.wait_ge(s_used, in_loop * 2 + (b - 1))
                nc.gpsimd.tensor_tensor(wlo[:, b % 2, :], raw[:, b % 2, :], whi[:, b % 2, :].bitcast(F32),
                                        ALU.subtract).then_inc(s_lo, 1)

            split(0)
            split(1)
            with pool.Fori(1, nblocks // 2) as i:
                split(0, i)
                split(1, i)
            if nblocks % 2:
                split(nblocks - 1)

        @block.scalar
        def _(act):
            ac = Chain(act, s_ac)

            def prep(b, i=None):
                if i is None:
                    if b >= nblocks:
                        return
                    act.wait_ge(s_raw[b % 2], 16 * (b // 2 + 1))
                    if b >= 2:
                        act.wait_ge(s_used, b - 1)
                else:
                    act.wait_ge(s_raw[b % 2], i * 16 + 16 * (b // 2 + 1))
                    wait(act, s_used, i * 2 + (b - 1))
                nc.scalar.activation(whi[:, b % 2, :], raw[:, b % 2, :], ACT.Copy).then_inc(s_hi, 1)

            def prep_run(b, n):
                if n >= 6:
                    with act.Fori(0, n // 2) as i:
                        prep(b + 1, i)
                        prep(b + 2, i)
                    if n % 2:
                        prep(b + n)
                else:
                    for j in range(n):
                        prep(b + 1 + j)

            def last_pair_run(b, n):
                if b + n < nblocks:
                    prep_run(b, n)
                else:
                    prep_run(b, n - 2)
                    prep(b + n - 1)

            def copy(dst, src, s, scale=1.0):
                nc.scalar.activation(dst, src, ACT.Copy, scale=scale).then_inc(s, 1)

            def rsqrt(dst, w, s):
                ac.link(nc.scalar.activation(dst, w, ACT.Ln, scale=-2.0))
                nc.scalar.activation(dst, dst, ACT.Exp, scale=-0.5).then_inc(s, 1)

            def norm(n, upd):
                nc.scalar.preload_act_table_set(LN_SET)
                for t in range(KT):
                    act.wait_ge(s_x, 8 * (upd - 1) + t + 1)
                    if 8 * n + t >= 2:
                        act.wait_ge(s_ss, 8 * n + t - 1)
                    nc.scalar.activation(sq[:, t % 2, :], xT[:, t, :], ACT.Square).then_inc(s_sq, 1)
                act.wait_ge(s_half, n + 1)
                rsqrt(rstd[:, :], t1[:, 0, :], s_rstd)
                if n == N_FINAL:
                    return
                for t in range(KT):
                    act.wait_ge(s_t1, 8 * hn(n) + t + 1)
                    nc.scalar.activation(hh[:, t, :], t1[:, t % 2, :], ACT.Copy).then_inc(s_hh, 1)

            def ffn(p):
                if p.half % 2 == 0:
                    norm(p.norm, p.upd)
                nc.scalar.preload_act_table_set(SILU_SET)
                func = ACT.Silu if p.swiglu else ACT.Relu

                def round_(i):
                    for j in range(2):
                        prep(p.b + j + 1, i)
                        if p.swiglu and j == 1:
                            continue
                        act.wait_ge(s_used, i * 2 + (p.b + j + 1))
                        for n in range(2):
                            wait(act, s_g, i * p.step + (p.tile + 2 * j + n - p.step + 1))
                            nc.scalar.activation(sg[:, 2 * j + n, :], ps[:, 2 * j + n, :], func)\
                                .then_inc(s_sg, 1)

                first = 0 if p.b else 1
                if first:
                    round_(0)
                with act.Fori(first, p.iters) as i:
                    round_(i)
                last_pair_run(p.b + p.up_blocks, p.down_blocks)

            act.dma_start(prow[PARAM_AT["ffn1_norm"]:PARAM_AT["ffn1_norm"] + 8, :],
                          dram["ffn1_norm"].rearrange("a (r c) -> (a r) c", c=P)).then_inc(s_in, 16)
            for name, rows in list(PARAM_ROWS.items())[1:]:
                v = dram[name]
                v = v.rearrange("(r c) -> r c", c=P) if len(v.shape) == 1 else \
                    v.rearrange("a (r c) -> (a r) c", c=P) if len(v.shape) == 2 else \
                    v.rearrange("a b (r c) -> (a b r) c", c=P)
                act.dma_start(prow[PARAM_AT[name]:PARAM_AT[name] + rows, :], v).then_inc(s_in, 16)
            act.dma_start(posi[:, :], dram["positions_2"][0].rearrange("(t p) -> p t", p=P),
                          allow_slow_non_contiguous=True).then_inc(s_in2, 16)
            for name, n in ROWP.items():
                act.dma_start(rowp[:, ROWP_AT[name]:ROWP_AT[name] + n],
                              dram[name][0:1, :].broadcast_to([P, n])).then_inc(s_in2, 16)
            act.wait_ge(s_vconst, NVC)
            act.dma_start(gate_w[0:16, 0, :], dram["gate_fwd_w"][0]).then_inc(s_in2, 16)
            act.dma_start(gate_w[16:32, 1, :], dram["gate_bwd_w"][0]).then_inc(s_in2, 16)
            prep(0)
            nc.scalar.preload_act_table_set(SILU_SET)
            act.wait_ge(s_ang, 1)
            nc.scalar.activation(sinr[:, :, :], rt[:, 0, :, :], ACT.Sin).then_inc(s_rope, 1)
            ac.link(nc.scalar.activation(rt[:, 1, :, :], rt[:, 0, :, :], ACT.Abs))
            nc.scalar.activation(cosr[:, :, :], rt[:, 1, :, :], ACT.Sin, bias=halfpi[:, :], scale=-1.0)\
                .then_inc(s_rope, 1)

            nc.scalar.preload_act_table_set(LN_SET)
            act.wait_ge(s_lam, 1)
            for c in range(2):
                nc.scalar.activation(lam[:, c:c + 1], lam[:, c:c + 1], ACT.Exp).then_inc(s_lam2, 1)

            def mix(b, upd):
                norm(N_MIX, upd)
                for j in range(MIX_BLOCKS):
                    prep(b + j + 1)
                    if j == 1:
                        act.wait_ge(s_mzg, 4)
                        ac.link(nc.scalar.activation(m_kin[:, :, :, :], m_g[:, :, :, :], ACT.Abs))
                        ac.link(nc.scalar.activation(m_kin[:, :, :, :], m_kin[:, :, :, :], ACT.Exp, scale=-1.0))
                        nc.scalar.activation(m_kin[:, :, :, :], m_kin[:, :, :, :], ACT.Ln, bias=one[:, :])\
                            .then_inc(s_mlog, 1)
                    if j == 2:
                        act.wait_ge(s_mscan, 4)
                        nc.scalar.preload_act_table_set(SILU_SET)
                        half = 0.5 / 16.0
                        nc.scalar.activation(m_qin[:, :, :, :], m_b[:, :, :, :], ACT.Sigmoid, scale=half)\
                            .then_inc(s_mexp, 1)
                        nc.scalar.activation(m_kin[:, :, :, :], m_b[:, :, :, :], ACT.Sigmoid, scale=-half)\
                            .then_inc(s_mexp, 1)
                    if j <= 10:
                        act.wait_ge(s_used, b + j + 1)
                    if j == 0:
                        copy(m_z[:, :], ps[:, 0, :], s_mz)
                    elif j in (1, 2):
                        for n in range(2):
                            copy((m_qT, m_kT)[j - 1][:, n, :], ps[:, 2 * j + n, :], s_mqk,
                                 GDK ** -0.5 if j == 1 else 1.0)
                    elif j == 4:
                        for n, bank in enumerate((0, 1, 6, 7)):
                            copy(m_v[:, n, :], ps[:, bank, :], s_mv)
                        for m, n in ((m_kin, 1), (m_qin, 3)):
                            act.wait_ge(s_mhalf, n)
                            nc.scalar.activation(m[:, :, :, :], m[:, :, :, :], ACT.Square).then_inc(s_mexp, 1)
                    elif j in (5, 6):
                        for n in range(2):
                            nc.scalar.activation(m_r[:, 2 * j - 10 + n, :], ps[:, 2 * j - 8 + n, :],
                                                 ACT.Silu).then_inc(s_mr, 1)
                        if j == 6:
                            nc.scalar.preload_act_table_set(LN_SET)
                    elif j in (7, 8):
                        for n in range(2):
                            copy(m_u[:, 2 * j - 14 + n, :], ps[:, 2 * j - 12 + n, :], s_mc)
                    elif j == 11:
                        for h in range(GH):
                            act.wait_ge(s_mo, h + 1)
                            if h >= 2:
                                act.wait_ge(s_mss, h - 1)
                            nc.scalar.activation(sq[:, h % 2, :], m_o[:, h, :], ACT.Square)\
                                .then_inc(s_mosq, 1)
                        for h in range(GH):
                            act.wait_ge(s_mvar, h + 1)
                            rsqrt(m_rstd[:, h, :], m_half[:, h, :], s_mrstd)
                    elif j == 12:
                        for k in range(KT):
                            act.wait_ge(s_mn, k + 1)
                            src = m_r[:, k, :] if k < GH else m_u[:, k - GH, :]
                            nc.scalar.activation(m_hi[:, k, :], src, ACT.Copy).then_inc(s_mhi, 1)
                last_pair_run(b + MIX_BLOCKS, OUT_BLOCKS)

            def xattn(b, upd):
                nc.scalar.preload_act_table_set(LN_SET)
                for t in range(KT):
                    act.wait_ge(s_xm, t + 1)
                    if t >= 2:
                        act.wait_ge(s_xmss, t - 1)
                    nc.scalar.activation(sq[:, t % 2, 0:NMEM], x_memT[:, t, :], ACT.Square).then_inc(s_xmsq, 1)
                act.wait_ge(s_xmvar, 1)
                rsqrt(rstd[:, 0:NMEM], t1[:, 0, 0:NMEM], s_xmrstd)
                for t in range(KT):
                    act.wait_ge(s_xmt1, t + 1)
                    nc.scalar.activation(x_mh[:, t, :], t1[:, t % 2, 0:NMEM], ACT.Copy).then_inc(s_xmh, 1)
                for j in range(4):
                    prep(b + j + 1)
                    act.wait_ge(s_used, b + j + 1)
                    for n in range(2):
                        copy(x_kT[:, 2 * j + n, :], ps[:, 2 * j + n, 0:NMEM], s_xk)
                for j in range(4, 8):
                    prep(b + j + 1)
                    if j % 2:
                        act.wait_ge(s_used, b + j + 1)
                        g = (j - 4) // 2
                        for m in range(MT):
                            copy(x_v[:, m, ts(g, 512)], ps[:, 1 + 2 * g + m, :], s_xv)
                norm(N_X, upd)
                for j in range(8, 12):
                    prep(b + j + 1)
                    act.wait_ge(s_used, b + j + 1)
                    for n in range(2):
                        copy(x_qT[:, 2 * (j - 8) + n, :], ps[:, 4 + 2 * (j % 2) + n, :], s_xq)
                for h in range(4):
                    act.wait_ge(s_xmax, h + 1)
                    if h >= 2:
                        act.wait_ge(s_xT, h - 1)
                    for qt in range(ST):
                        c = 4 * h + qt
                        nc.scalar.activation(x_p[:, h % 2, qt, :],
                                             ps[:, 2 * (h % 2) + qt // 2, (qt % 2) * NMEM:(qt % 2 + 1) * NMEM],
                                             ACT.Exp, bias=small[:, c:c + 1], scale=1.0 / 16.0,
                                             accum_out=small[:, 16 + c:17 + c]).then_inc(s_xe, 1)
                    act.wait_ge(s_xT, h + 1)
                    if h >= 2:
                        act.wait_ge(s_xo, h - 1)
                    for m in range(MT):
                        copy(x_pT[:, h % 2, m, :], ps[:, 4 + m, :], s_xpT)
                last_pair_run(b + X_BLOCKS, OUT_BLOCKS)

            def row_bank(k, dst, sqr=True, scale=1.0):
                act.wait_ge(*row_bank_ready(k))
                if sqr:
                    nc.scalar.activation(a_sq[:, k % 4, :], ps[:, k % 4, :], ACT.Square)
                nc.scalar.activation(dst, ps[:, k % 4, :], ACT.Copy, scale=scale).then_inc(s_rcopy, 1)

            def row_rstd(g):
                act.wait_ge(s_rvar, g + 1)
                rsqrt(small[:, 0:32], newton[:, 0, 0:32], s_rrs)

            def turned(k, n, dst):
                for j in range(n):
                    act.wait_ge(s_rt, k + j + 1)
                    copy(dst(j), ps[:, 4 + (k + j) % 4, :], s_rtc)

            def diff(b, upd):
                norm(N_DIFF, upd)
                for g in range(6):
                    for j in range(2):
                        prep(b + 2 * g + j + 1)
                        if j == 0 and 1 <= g <= 4:
                            turned(4 * (g - 1), 4,
                                   lambda c: ((a_qT if g <= 2 else a_kT)[:, 4 * ((g - 1) % 2) + c, :]))
                    for st in range(ST):
                        if g < 4:
                            if st == 0 and g >= 1:
                                act.wait_ge(s_rss, g)
                            if st == 0 and g >= 2:
                                act.wait_ge(s_rt, 4 * (g - 1))
                            row_bank(4 * g + st, a_rows[:, g % 2, st, :])
                        else:
                            row_bank(4 * g + st, a_v[:, st, ts(g - 4, 512)], False)
                    if g < 4:
                        row_rstd(g)
                for u in range(32):
                    h, qt = divmod(u, 4)
                    nk = P * (qt + 1)
                    act.wait_ge(s_dmax, u + 1)
                    if u >= 2:
                        act.wait_ge(s_da, u - 1)
                    for c in range(2):
                        nc.scalar.activation(d_p[:, u % 2, c, 0:nk], ps[:, 2 * (u % 2) + c, 0:nk], ACT.Exp,
                                             bias=small[:, 2 * (u % 2) + c:2 * (u % 2) + c + 1], scale=-1.0,
                                             accum_out=small[:, 4 + 2 * (u % 2) + c:5 + 2 * (u % 2) + c])\
                            .then_inc(s_de, 1)
                    if u >= 1:
                        pT_copy(u - 1)
                    if h >= 1 and qt == 3:
                        d_squares(h - 1)
                    if h >= 2 and qt == 0:
                        d_rstd(h - 2)
                pT_copy(31)
                d_rstd(6)
                d_squares(7)
                d_rstd(7)
                last_pair_run(b + DIFF_BLOCKS, OUT_BLOCKS)

            def pT_copy(u):
                nk = P * (u % 4 + 1)
                act.wait_ge(s_dT, u + 1)
                if u >= 2:
                    act.wait_ge(s_dpv, u - 1)
                copy(d_aT[:, u % 2, 0:nk], ps[:, 4 + u % 2, 0:nk], s_daT)

            def d_squares(h):
                act.wait_ge(s_dor, h + 1)
                if h >= 1:
                    act.wait_ge(s_doss, h)
                nc.scalar.activation(d_osq[:, :], d_o[:, h % 2, :], ACT.Square).then_inc(s_dosq, 1)

            def d_rstd(h):
                act.wait_ge(s_dovar, h + 1)
                if h:
                    act.wait_ge(s_don, h)
                rsqrt(small[:, 20:24], newton[:, 0, 0:4], s_dors)

            def dsa(b, upd):
                norm(N_DSA, upd)
                k0 = 24
                prep(b + 1)
                for st in range(ST):
                    act.wait_ge(*row_bank_ready(k0 + st))
                    nc.scalar.activation(a_sq[:, st, 0:256], ps[:, st, 0:256], ACT.Square,
                                         accum_out=small[:, 32 + st:33 + st]).then_inc(s_ccq, 1)
                    nc.scalar.activation(c_cq[:, st, :], ps[:, st, 0:256], ACT.Copy).then_inc(s_rcopy, 1)
                act.wait_ge(s_rvar, 5)
                rsqrt(small[:, 36:40], newton[:, 0, 0:4], s_ccqr)
                prep(b + 2)
                for st in range(ST):
                    act.wait_ge(*row_bank_ready(k0 + 4 + st))
                    nc.scalar.activation(a_sq[:, st, 0:64], ps[:, st, 0:64], ACT.Square,
                                         accum_out=small[:, 40 + st:41 + st]).then_inc(s_cid, 1)
                    nc.scalar.activation(small[:, 8 * st:8 * st + 8], ps[:, st, 64:72], ACT.Copy,
                                         scale=(IH * 64) ** -0.5)
                    nc.scalar.activation(c_kid[:, st, 0:64], ps[:, st, 0:64], ACT.Copy).then_inc(s_rcopy, 1)
                act.wait_ge(s_rvar, 6)
                rsqrt(small[:, 44:48], newton[:, 0, 0:4], s_cidr)
                for k in range(2):
                    act.wait_ge(s_cqT, k + 1)
                    nc.scalar.activation(c_cqh[:, k, :], ps[:, 4 + k, :], ACT.Copy).then_inc(s_cqh, 1)
                act.wait_ge(s_ckT, 1)
                copy(c_kiT[:, :], ps[:, 6, :], s_ckTc)
                prep(b + 3)
                prep(b + 4)
                for st in range(ST):
                    row_bank(k0 + 8 + st, a_rows[:, 0, st, :])
                row_rstd2(0)
                prep(b + 5)
                for st in range(ST):
                    row_bank(k0 + 12 + st, a_rows[:, 1, st, :], False)
                turned(16, 4, lambda c: c_qiT[:, c, :])
                for v in range(32):
                    qt, h = divmod(v, IH)
                    nk = P * (qt + 1)
                    act.wait_ge(s_cdot, v + 1)
                    if v >= 2:
                        act.wait_ge(s_cacc, v - 1)
                    nc.scalar.activation(c_relu[:, v % 2, 0:nk], ps[:, 4 + v % 4, 0:nk], ACT.Relu)\
                        .then_inc(s_crelu, 1)
                prep(b + 6)
                turned(20, 4, lambda c: a_kT[:, c, :])
                act.wait_ge(s_rss2, 1)
                for st in range(ST):
                    row_bank(k0 + 16 + st, a_rows[:, 0, st, :])
                row_rstd2(1)
                act.wait_ge(s_rss2, 2)
                for st in range(ST):
                    row_bank(k0 + 20 + st, a_rows[:, 1, st, :])
                row_rstd2(2)
                prep(b + 7)
                prep(b + 8)
                turned(24, 4, lambda c: a_qT[:, c, :])
                act.wait_ge(s_rss2, 3)
                for st in range(ST):
                    row_bank(k0 + 24 + st, a_rows[:, 0, st, :])
                row_rstd2(3)
                turned(28, 4, lambda c: a_qT[:, 4 + c, :])
                for g in range(2):
                    prep(b + 9 + 2 * g)
                    prep(b + 10 + 2 * g)
                    for st in range(ST):
                        row_bank(k0 + 28 + 4 * g + st, a_v[:, st, ts(g, 512)], False)
                turned(32, 4, lambda c: a_kT[:, 4 + c, :])
                for u in range(64):
                    nk = P * (u % 4 + 1)
                    act.wait_ge(s_cs, u + 1)
                    if u >= 2:
                        act.wait_ge(s_cT, u - 1)
                    if u >= 16:
                        act.wait_ge(s_cor, u // 8 - 1)
                    k = 16 + u % 16
                    nc.scalar.activation(c_p[:, u % 2, 0:nk], c_s[:, u % 4, 0:nk], ACT.Exp,
                                         bias=small[:, u % 4:u % 4 + 1], scale=-1.0,
                                         accum_out=small[:, k:k + 1]).then_inc(s_ce, 1)
                    if u >= 1:
                        c_copy(u - 1)
                c_copy(63)
                last_pair_run(b + DSA_BLOCKS, OUT_BLOCKS)

            def row_rstd2(g):
                act.wait_ge(s_rvar, 7 + g)
                rsqrt(c_rs[:, 0:32], newton[:, 0, 0:32], s_rrs2)

            def c_copy(u):
                if u % 2:
                    return
                nk = P * (u % 4 + 1)
                act.wait_ge(s_cT, u + 1)
                if u >= 2:
                    act.wait_ge(s_cpv, u - 1)
                copy(c_pT[:, u % 2, 0:nk], ps[:, 4 + u % 2, 0:nk], s_cpTa)

            for stage in stages:
                if isinstance(stage, Pass):
                    ffn(stage)
                elif stage == "final":
                    norm(N_FINAL, at["final"][1])
                else:
                    {"mix": mix, "x": xattn, "diff": diff, "dsa": dsa}[stage[0]](*at[stage[0]][:2])
            for k in range(1, 2 * ST, 2):
                act.wait_ge(s_ot, k + 1)
                copy(orows[:, k // 2, ts(k % 2, 512)], ps[:, k, :], s_orow)

        @block.tensor
        def _(pe):
            def mm3(dst, w_hi, w_lo, x_hi, x_lo, start, stop):
                nc.tensor.matmul(dst, w_hi, x_hi, start=start, stop=False)
                nc.tensor.matmul(dst, w_hi, x_lo, start=False, stop=False)
                return nc.tensor.matmul(dst, w_lo, x_hi, start=False, stop=stop)

            def use(b, i=None):
                pe.wait_ge(s_lo, b + 1 if i is None else i * 2 + (b + 1))

            def up_block(b, i, banks, xh, xl, n, ready=None, width=2):
                use(b, i)
                w = b % 2
                for k in range(KT):
                    if ready is not None:
                        pe.wait_ge(*ready(k))
                    for j in range(width):
                        c = slice(k * 256 + j * P, k * 256 + (j + 1) * P)
                        r = mm3(ps[:, banks[j], 0:n], whi[:, w, c], wlo[:, w, c], xh[:, k, 0:n], xl[:, k, 0:n],
                                k == 0, k == KT - 1)
                r.then_inc(s_used, 1)

            def down_block(b, i, gi, first, last):
                use(b, i)
                w = b % 2
                for n in range(KT):
                    for k in range(2):
                        c = slice(k * D + n * P, k * D + (n + 1) * P)
                        r = mm3(ps[:, n, :], whi[:, w, c], wlo[:, w, c], gh[:, ds(gi + k, 1), :],
                                gl[:, ds(gi + k, 1), :], first and k == 0, last and k == 1)
                    if last and n < KT - 1:
                        r.then_inc(s_down, 1)
                r.then_inc(s_used, 1)

            def norm(n):
                for t in range(KT):
                    pe.wait_ge(s_sq, 8 * n + t + 1)
                    nc.tensor.matmul(ps[:, 0, :], ones[:, :], sq[:, t % 2, :], start=t == 0, stop=t == KT - 1)\
                        .then_inc(s_ss, 1)

            def normed(n):
                return lambda k: (s_hl, 8 * hn(n) + k + 1)

            def ffn(p):
                if p.half % 2 == 0:
                    norm(p.norm)
                    pe.wait_ge(s_rstd, p.norm + 1)

                def round_(i):
                    t = p.tile - p.step + 2
                    wait(pe, s_sg, i * p.step + t)
                    wait(pe, s_x, 8 * p.upd)
                    up_block(p.b, i, (0, 1), hh, hl, S, normed(p.norm))
                    if p.swiglu:
                        wait(pe, s_g, i * p.step + t)
                    else:
                        wait(pe, s_sg, i * p.step + t + 2)
                    up_block(p.b + 1, i, (2, 3), hh, hl, S)

                first = 0 if p.b else 1
                if first:
                    round_(0)
                with pe.Fori(first, p.iters) as i:
                    round_(i)
                b, n = p.b + p.up_blocks, p.down_blocks
                pe.wait_ge(s_g, p.tile + p.tiles)
                pe.wait_ge(s_sg, p.tile + p.tiles)
                down_block(b, None, 0, True, False)
                pairs = (n - 2) // 2
                with pe.Fori(0, pairs) as i:
                    down_block(b + 1, i, i * 4 + 2, False, False)
                    down_block(b + 2, i, i * 4 + 4, False, False)
                for j in range(1 + 2 * pairs, n):
                    down_block(b + j, None, 2 * j, False, j == n - 1)

            def project_out(b, upd, ready, xh=hh, xl=hl):
                for j in range(OUT_BLOCKS):
                    use(b + j)
                    w = (b + j) % 2
                    for k in range(KT):
                        if j == 0:
                            pe.wait_ge(*ready(k))
                        for n in range(2):
                            c = slice(k * 256 + n * P, k * 256 + (n + 1) * P)
                            r = mm3(ps[:, 2 * j + n, :], whi[:, w, c], wlo[:, w, c], xh[:, k, :], xl[:, k, :],
                                    k == 0, k == KT - 1)
                            if k == KT - 1:
                                r.then_inc((s_down, s_used)[n], 1)

            pe.wait_ge(s_const, 1)
            pe.wait_ge(s_in, 16 * (1 + len(PARAM_ROWS)))
            nc.tensor.transpose(ps[:, 7, 0:NPARAM], prow[:, :], ident[0:NPARAM, 0:NPARAM]).then_inc(s_tr0, 1)
            for t in range(KT):
                if t == 7:
                    pe.wait_ge(s_par, 1)
                for st in range(ST):
                    r = nc.tensor.transpose(ps[:, t, ts(st, P)], xrows[:, st, ts(t, P)], ident[:, :])
                r.then_inc(s_tr0, 1)

            def mix(b, upd):
                norm(N_MIX)
                pe.wait_ge(s_rstd, N_MIX + 1)
                up_block(b, None, (0,), hh, hl, S, normed(N_MIX), width=1)
                pe.wait_ge(s_mz, 1)
                for d in range(2):
                    for j in range(2):
                        nc.tensor.matmul(ps[:, (0, 1, 6, 7)[2 * d + j], :], gate_w[:, d, ts(j, P)], m_z[0:ZW, :],
                                         start=True, stop=True).then_inc(s_mgate, 1)
                up_block(b + 1, None, (2, 3), hh, hl, S)
                up_block(b + 2, None, (4, 5), hh, hl, S)
                pe.wait_ge(s_mzg, 4)
                for j in range(2):
                    use(b + 3 + j)
                    w = (b + 3 + j) % 2
                    for st in range(ST):
                        for k in range(4):
                            kk = 4 * j + k
                            r = mm3(ps[:, (0, 1, 6, 7)[st], :], hh[:, kk, ts(st, P)], hl[:, kk, ts(st, P)],
                                    whi[:, w, ts(k, S)], wlo[:, w, ts(k, S)], kk == 0, kk == KT - 1)
                    r.then_inc(s_used, 1)
                pe.wait_ge(s_mqk, 2)
                up_block(b + 5, None, (2, 3), hh, hl, S)
                pe.wait_ge(s_mv, 4)
                pe.wait_ge(s_mkin, 5)
                for d in range(2):
                    for j in range(2):
                        for st in range(ST):
                            r = nc.tensor.transpose(ps[:, (0, 1, 6, 7)[2 * d + j], ts(st, P)],
                                                    m_kst[:, d, j, ts(st, P)], ident[:, :])
                        r.then_inc(s_mkt, 1)
                pe.wait_ge(s_mqk, 4)
                up_block(b + 6, None, (4, 5), hh, hl, S)

                def chunk_sums(d):
                    pe.wait_ge(s_mktc, 4)
                    if d:
                        pe.wait_ge(s_mst, 14)
                    for j in range(2):
                        for n in range(NCH):
                            rows = slice(CH * (n % 2), CH * (n % 2) + CH)
                            for h in range(2):
                                r = nc.tensor.matmul(
                                    ps[CH * h:CH * h + CH, (0, 1, 6, 7)[2 * j + n % 2], ts(n // 2, GDV)],
                                    m_kst_row[rows, d, j, n // 2, CH * h:CH * h + CH],
                                    m_v[rows, n // 2, ts(2 * j + h, GDV)], start=True, stop=True)
                        r.then_inc(s_mds, 1)

                chunk_sums(0)
                pe.wait_ge(s_mr, 2)
                up_block(b + 7, None, (2, 3), hh, hl, S)
                chunk_sums(1)
                pe.wait_ge(s_mr, 4)
                up_block(b + 8, None, (4, 5), hh, hl, S)

                def products(h):
                    pe.wait_ge(s_mst, 28)
                    if h >= 2:
                        pe.wait_ge(s_matc, h - 1)
                    rows = slice(CH * (h % 2), CH * (h % 2) + CH)
                    for d in range(2):
                        for st in range(ST):
                            r = nc.tensor.matmul(ps[:, (0, 1, 6, 7)[2 * (h % 2) + d], ts(st, P)],
                                                 m_kin[rows, d, h // 2, ts(st, P)],
                                                 m_qin[rows, d, h // 2, ts(st, P)], start=True, stop=True)
                    r.then_inc(s_matt, 1)

                products(0)
                products(1)
                pe.wait_ge(s_mc, 2)
                up_block(b + 9, None, (2, 3), hh, hl, S)
                products(2)
                products(3)
                pe.wait_ge(s_mc, 4)
                up_block(b + 10, None, (4, 5), hh, hl, S)
                pe.wait_ge(s_matc, 4)

                def squares(h):
                    pe.wait_ge(s_mosq, h + 1)
                    nc.tensor.matmul(ps[:, (0, 1, 6, 7)[h], :], ones[:, :], sq[:, h % 2, :],
                                     start=True, stop=True).then_inc(s_mss, 1)

                for h in range(GH):
                    bank, rows = (0, 1, 6, 7)[h], slice(CH * (h % 2), CH * (h % 2) + CH)
                    for st in range(ST):
                        nc.tensor.matmul(ps[:, bank, ts(st, P)], m_v[:, st, ts(h, GDV)], m_att[:, h, ts(st, P)],
                                         start=st == 0, stop=False, skip_group_check=True)
                    for d in range(2):
                        for n in (range(1, NCH), range(NCH - 1))[d]:
                            r = nc.tensor.matmul(ps[:, bank, ts(n, CH)], m_state[rows, d, h // 2, n, :],
                                                 m_qin[rows, d, h // 2, ts(n, CH)], start=False,
                                                 stop=d == 1, skip_group_check=True)
                    r.then_inc(s_mot, 1)
                    if h:
                        squares(h - 1)
                squares(3)
                pe.wait_ge(s_mu, 2)
                up_block(b + 11, None, (2, 3), hh, hl, S)
                pe.wait_ge(s_mu, 4)
                up_block(b + 12, None, (4, 5), hh, hl, S)
                project_out(b + MIX_BLOCKS, upd, lambda k: (s_mfin, k + 1), m_hi, m_lo)

            def xattn(b, upd):
                pe.wait_ge(s_memrow, 16)
                pe.wait_ge(s_x, 8 * upd)
                for t in range(KT):
                    if t >= 4:
                        pe.wait_ge(s_xm, t - 3)
                    for m in range(MT):
                        r = nc.tensor.transpose(ps[:, 4 + t % 4, ts(m, P)], x_mrow[:, m, ts(t, P)], ident[:, :])
                    r.then_inc(s_xmT, 1)
                for t in range(KT):
                    pe.wait_ge(s_xmsq, t + 1)
                    nc.tensor.matmul(ps[:, 0, 0:NMEM], ones[:, :], sq[:, t % 2, 0:NMEM], start=t == 0,
                                     stop=t == KT - 1).then_inc(s_xmss, 1)
                pe.wait_ge(s_xmrstd, 1)
                for j in range(4):
                    up_block(b + j, None, (2 * j, 2 * j + 1), x_mh, x_ml, NMEM, lambda k: (s_xml, k + 1))
                for g in range(2):
                    pe.wait_ge(s_xk, 2 + 2 * g + 1)
                    for j in range(2):
                        bb = b + 4 + 2 * g + j
                        use(bb)
                        w = bb % 2
                        for m in range(MT):
                            for k in range(4):
                                kk = 4 * j + k
                                r = mm3(ps[:, 1 + 2 * g + m, :], x_mh[:, kk, ts(m, P)], x_ml[:, kk, ts(m, P)],
                                        whi[:, w, ts(k, S)], wlo[:, w, ts(k, S)], kk == 0, kk == KT - 1)
                        r.then_inc(s_used, 1)
                norm(N_X)
                for j in range(4):
                    if j < 2:
                        pe.wait_ge(s_xk, 8)
                        pe.wait_ge(s_xv, 4)
                    else:
                        pe.wait_ge(s_xq, 2 * j - 2)
                    up_block(b + 8 + j, None, (4 + 2 * (j % 2), 5 + 2 * (j % 2)), hh, hl, S, normed(N_X))
                pe.wait_ge(s_xq, 8)
                pe.wait_ge(s_rstd, N_X + 1)

                def scores(h):
                    if h >= 2:
                        pe.wait_ge(s_xe, 4 * (h - 1))
                    for qt in range(ST):
                        for k in range(2):
                            r = nc.tensor.matmul(ps[:, 2 * (h % 2) + qt // 2, ts(qt % 2, NMEM)],
                                                 x_qT[:, 2 * h + k, ts(qt, P)], x_kT[:, 2 * h + k, :],
                                                 start=k == 0, stop=k == 1)
                    r.then_inc(s_xs, 1)

                def weigh(h):
                    if h:
                        pe.wait_ge(s_xol, 2 * h)
                    pe.wait_ge(s_xpT, 2 * h + 2)
                    for e in range(2):
                        for m in range(MT):
                            r = nc.tensor.matmul(ps[:, 6 + e, :], x_v[:, m, ts(2 * h + e, P)],
                                                 x_pT[:, h % 2, m, :], start=m == 0, stop=m == MT - 1)
                    r.then_inc(s_xo, 1)

                scores(0)
                for h in range(4):
                    if h < 3:
                        scores(h + 1)
                    pe.wait_ge(s_xn, h + 1)
                    if h:
                        pe.wait_ge(s_xpT, 2 * h)
                    for m in range(MT):
                        for qt in range(ST):
                            r = nc.tensor.transpose(ps[:, 4 + m, ts(qt, P)], x_p[:, h % 2, qt, ts(m, P)],
                                                    ident[:, :])
                    r.then_inc(s_xT, 1)
                    if h:
                        weigh(h - 1)
                weigh(3)
                pe.wait_ge(s_xe, 16)
                pe.wait_ge(s_xol, 8)
                project_out(b + X_BLOCKS, upd, lambda k: (s_xol, 8))

            def row_group(b, r0, xh, xl, kt, wcols, blocks, ready=None):
                kb, n = kt // blocks, wcols.stop - wcols.start
                for j in range(blocks):
                    use(b + j)
                    w = (b + j) % 2
                    wide = whi[:, w, :].rearrange("p (k n) -> p k n", k=kb)
                    wide_lo = wlo[:, w, :].rearrange("p (k n) -> p k n", k=kb)
                    by_tile = ready is not None
                    for a in range(kb if by_tile else ST):
                        for c in range(ST if by_tile else kb):
                            k, st = (a, c) if by_tile else (c, a)
                            if by_tile and c == 0:
                                pe.wait_ge(*ready(j * kb + k))
                            if j == 0 and k == 0 and r0 + st >= 4:
                                pe.wait_ge(s_rcopy, r0 + st - 3)
                            kk = j * kb + k
                            r = mm3(ps[:, st, 0:n], xh[:, kk, ts(st, P)], xl[:, kk, ts(st, P)],
                                    wide[:, k, wcols], wide_lo[:, k, wcols], kk == 0, kk == kt - 1)
                            if k == kb - 1:
                                if st == ST - 1:
                                    r.then_inc(s_used, 1)
                                elif j == blocks - 1:
                                    r.then_inc(s_rb, 1)

            def turn_rows(k0, slot):
                for c in range(4):
                    if k0 + c >= 4:
                        pe.wait_ge(s_rtc, k0 + c - 3)
                    for st in range(ST):
                        r = nc.tensor.transpose(ps[:, 4 + c, ts(st, P)], a_rows[:, slot, st, ts(c, P)],
                                                ident[:, :])
                    r.then_inc(s_rt, 1)

            def diff(b, upd):
                norm(N_DIFF)
                pe.wait_ge(s_rstd, N_DIFF + 1)
                for g in range(6):
                    if 1 <= g <= 4:
                        half_group(b + 2 * g, 4 * g, 0)
                        pe.wait_ge(s_rows, g)
                        turn_rows(4 * (g - 1), (g - 1) % 2)
                        half_group(b + 2 * g + 1, 4 * g, 1)
                    else:
                        row_group(b + 2 * g, 4 * g, hh, hl, KT, slice(0, 512), 2, normed(N_DIFF) if g == 0 else None)
                pe.wait_ge(s_rtc, 16)
                pe.wait_ge(s_rcopy, 24)

                def scores(u):
                    h, qt = divmod(u, 4)
                    if u >= 2:
                        pe.wait_ge(s_de, 2 * (u - 1))
                    for c in range(2):
                        rows = slice(64 * c, 64 * c + 64)
                        r = nc.tensor.matmul(ps[:, 2 * (u % 2) + c, 0:P * (qt + 1)],
                                             a_qT[rows, h, ts(qt, P)], a_kT[rows, h, 0:P * (qt + 1)],
                                             start=True, stop=True)
                    r.then_inc(s_ds, 1)

                def turn_out(h):
                    pe.wait_ge(s_don, h + 1)
                    for st in range(ST):
                        r = nc.tensor.transpose(ps[:, 6 + h % 2, ts(st, P)], d_o[:, h % 2, ts(st, P)],
                                                ident[:, :])
                    r.then_inc(s_doT, 1)

                def weigh(u):
                    h, qt = divmod(u, 4)
                    pe.wait_ge(s_daT, u + 1)
                    if h >= 2 and qt == 0:
                        pe.wait_ge(s_dhl, h - 1)
                    for kb in range(qt + 1):
                        r = nc.tensor.matmul(ps[:, 6 + h % 2, ts(qt, P)], d_aT[:, u % 2, ts(kb, P)],
                                             a_v[:, kb, ts(h, P)], start=kb == 0, stop=kb == qt)
                    r.then_inc(s_dpv, 1)

                scores(0)
                scores(1)
                for u in range(32):
                    h, qt = divmod(u, 4)
                    pe.wait_ge(s_da, u + 1)
                    if u >= 2:
                        pe.wait_ge(s_daT, u - 1)
                    for kb in range(qt + 1):
                        r = nc.tensor.transpose(ps[:, 4 + u % 2, ts(kb, P)], d_a[:, u % 2, ts(kb, P)],
                                                ident[:, :])
                    r.then_inc(s_dT, 1)
                    if u < 30:
                        scores(u + 2)
                    if qt == 0 and h >= 2:
                        turn_out(h - 2)
                    if u:
                        weigh(u - 1)
                weigh(31)
                turn_out(6)
                turn_out(7)
                pe.wait_ge(s_dhl, 8)
                pe.wait_ge(s_daT, 32)
                pe.wait_ge(s_dor, 8)
                project_out(b + DIFF_BLOCKS, upd, lambda k: (s_dhl, 8))

            def half_group(b, r0, j):
                use(b)
                w = b % 2
                for st in range(ST):
                    if j == 0 and r0 + st >= 4:
                        pe.wait_ge(s_rcopy, r0 + st - 3)
                    for k in range(4):
                        kk = 4 * j + k
                        r = mm3(ps[:, st, :], hh[:, kk, ts(st, P)], hl[:, kk, ts(st, P)],
                                whi[:, w, ts(k, S)], wlo[:, w, ts(k, S)], kk == 0, kk == KT - 1)
                    if st == ST - 1:
                        r.then_inc(s_used, 1)
                    elif j == 1:
                        r.then_inc(s_rb, 1)

            def dsa(b, upd):
                r0 = 24
                norm(N_DSA)
                pe.wait_ge(s_rstd, N_DSA + 1)
                row_group(b, r0, hh, hl, KT, slice(0, 256), 1, normed(N_DSA))
                row_group(b + 1, r0 + 4, hh, hl, KT, slice(184, 256), 1)
                pe.wait_ge(s_ccqn, 1)
                for k in range(2):
                    for st in range(ST):
                        r = nc.tensor.transpose(ps[:, 4 + k, ts(st, P)], c_cq[:, st, ts(k, P)], ident[:, :])
                    r.then_inc(s_cqT, 1)
                pe.wait_ge(s_cidn, 1)
                for st in range(ST):
                    r = nc.tensor.transpose(ps[:, 6, ts(st, P)], c_kid[:, st, :], ident[:, :])
                r.then_inc(s_ckT, 1)
                row_group(b + 2, r0 + 8, hh, hl, KT, slice(0, 512), 2)
                pe.wait_ge(s_cql, 2)
                compressed(b + 4, r0 + 12, 1)
                pe.wait_ge(s_ckTc, 1)
                pe.wait_ge(s_rows, 6)
                turn_rows(16, 1)
                pe.wait_ge(s_rtc, 20)
                for v in range(32):
                    qt, h = divmod(v, IH)
                    if v >= 4:
                        pe.wait_ge(s_crelu, v - 3)
                    rows = slice(64 * (h % 2), 64 * (h % 2) + 64)
                    nc.tensor.matmul(ps[:, 4 + v % 4, 0:P * (qt + 1)], c_qiT[rows, h // 2, ts(qt, P)],
                                     c_kiT[rows, 0:P * (qt + 1)], start=True, stop=True).then_inc(s_cdot, 1)
                pe.wait_ge(s_crelu, 32)
                turn_rows(20, 0)
                compressed(b + 5, r0 + 16, 2)
                half_group(b + 6, r0 + 24, 0)
                pe.wait_ge(s_rows, 7)
                turn_rows(24, 0)
                half_group(b + 7, r0 + 24, 1)
                pe.wait_ge(s_rows, 8)
                turn_rows(28, 1)
                row_group(b + 8, r0 + 28, hh, hl, KT, slice(0, 512), 2)
                row_group(b + 10, r0 + 32, hh, hl, KT, slice(0, 512), 2)
                pe.wait_ge(s_rows, 9)
                turn_rows(32, 0)
                pe.wait_ge(s_rtc, 36)
                pe.wait_ge(s_rcopy, r0 + 36)

                def scores(u):
                    h, qt = divmod(u, 4)
                    if u >= 4:
                        pe.wait_ge(s_cs, u - 3)
                    rows = slice(64 * (h % 2), 64 * (h % 2) + 64)
                    nc.tensor.matmul(ps[:, u % 4, 0:P * (qt + 1)], a_qT[rows, h // 2, ts(qt, P)],
                                     a_kT[rows, h // 2, 0:P * (qt + 1)], start=True, stop=True)\
                        .then_inc(s_cs0, 1)

                def turn_out(j):
                    pe.wait_ge(s_cor, j + 1)
                    for st in range(ST):
                        r = nc.tensor.transpose(ps[:, 6 + j % 2, ts(st, P)], c_o[:, j % 2, ts(st, P)], ident[:, :])
                    r.then_inc(s_coT, 1)

                def weigh(u):
                    h, qt = divmod(u, 4)
                    pe.wait_ge(*pT_copied(u))
                    if u % 8 == 0 and u >= 16:
                        pe.wait_ge(s_chl, u // 8 - 1)
                    for kb in range(qt + 1):
                        c = qt * P + 64 * (h % 2)
                        r = nc.tensor.matmul(ps[:, 6 + h // 2 % 2, c:c + 64], c_pT[:, u % 2, ts(kb, P)],
                                             a_v[:, kb, ts(h, 64)], start=kb == 0, stop=kb == qt)
                    r.then_inc(s_cpv, 1)

                for u in range(3):
                    scores(u)
                for u in range(64):
                    h, qt = divmod(u, 4)
                    pe.wait_ge(s_ce, u + 1)
                    if u >= 2:
                        pe.wait_ge(*pT_copied(u - 2))
                    for kb in range(qt + 1):
                        r = nc.tensor.transpose(ps[:, 4 + u % 2, ts(kb, P)], c_p[:, u % 2, ts(kb, P)],
                                                ident[:, :])
                    r.then_inc(s_cT, 1)
                    if u < 61:
                        scores(u + 3)
                    if u % 8 == 3 and u > 8:
                        turn_out(u // 8 - 1)
                    if u:
                        weigh(u - 1)
                weigh(63)
                turn_out(7)
                pe.wait_ge(s_chl, 8)
                pe.wait_ge(*pT_copied(62))
                pe.wait_ge(*pT_copied(63))
                pe.wait_ge(s_cor, 8)
                project_out(b + DSA_BLOCKS, upd, lambda k: (s_chl, 8))

            def pT_copied(u):
                return (s_cpTd if u % 2 else s_cpTa, u // 2 + 1)

            def compressed(b, r0, groups):
                use(b)
                w = b % 2
                for g in range(groups):
                    for st in range(ST):
                        pe.wait_ge(s_rcopy, r0 + 4 * g + st - 3)
                        for k in range(2):
                            c = slice(k * 512 * groups + g * 512, k * 512 * groups + (g + 1) * 512)
                            r = mm3(ps[:, st, :], c_cqh[:, k, ts(st, P)], c_cql[:, k, ts(st, P)],
                                    whi[:, w, c], wlo[:, w, c], k == 0, k == 1)
                        r.then_inc(s_used if g == groups - 1 and st == ST - 1 else s_rb, 1)

            for stage in stages:
                if isinstance(stage, Pass):
                    ffn(stage)
                elif stage == "final":
                    norm(N_FINAL)
                else:
                    {"mix": mix, "x": xattn, "diff": diff, "dsa": dsa}[stage[0]](*at[stage[0]][:2])
            for st in range(ST):
                for half in range(2):
                    for t in range(4):
                        pe.wait_ge(s_x, 8 * (nupd - 1) + 4 * half + t + 1)
                        r = nc.tensor.transpose(ps[:, 2 * st + half, ts(t, P)], xT[:, 4 * half + t, ts(st, P)],
                                                ident[:, :])
                    r.then_inc(s_ot, 1)

        @block.vector
        def _(dve):
            V = nc.vector
            dv = Chain(dve, s_dv)

            def split_lo(dst, src, hi, s):
                V.tensor_tensor(dst, src, hi.bitcast(F32), ALU.subtract).then_inc(s, 1)

            def half(w, ss, n, s):
                V.tensor_scalar(w, ss, -0.5 / n, -0.5 * EPS, ALU.mult, ALU.add).then_inc(s, 1)

            def refine(y, w, u):
                dv.link(V.tensor_tensor(u, y, y, ALU.mult))
                dv.link(V.tensor_tensor(w, w, u, ALU.mult))
                dv.link(V.scalar_tensor_tensor(out=y, in0=w, scalar=1.5, in1=y, op0=ALU.add, op1=ALU.mult))

            def norm(n, upd):
                name, g0 = NORM_GAIN[n]
                dve.wait_ge(s_ss, 8 * n + 8)
                half(t1[:, 0, :], ps[:, 0, :], D, s_half)
                dve.wait_ge(s_rstd, n + 1)
                refine(rstd[:, :], t1[:, 0, :], t1[:, 1, :])
                if n == N_FINAL:
                    for t in range(KT):
                        V.scalar_tensor_tensor(out=xT[:, t, :], in0=xT[:, t, :], scalar=col(name, g0 + t),
                                               in1=rstd[:, :], op0=ALU.mult, op1=ALU.mult).then_inc(s_x, 1)
                    return

                def lo(t):
                    dve.wait_ge(s_hh, 8 * hn(n) + t + 1)
                    split_lo(hl[:, t, :], t1[:, t % 2, :], hh[:, t, :], s_hl)

                for t in range(KT):
                    if t >= 2:
                        dve.wait_ge(s_hl, 8 * hn(n) + t - 1)
                    V.scalar_tensor_tensor(out=t1[:, t % 2, :], in0=xT[:, t, :], scalar=col(name, g0 + t),
                                           in1=rstd[:, :], op0=ALU.mult, op1=ALU.mult).then_inc(s_t1, 1)
                    if t:
                        lo(t - 1)
                lo(KT - 1)

            def update(down, b_last, out, scale=1.0):
                for n in range(KT):
                    if out:
                        dve.wait_ge(*((s_used, b_last - 3 + n // 2 + 1) if n % 2 else (s_down, down + n // 2 + 1)))
                    else:
                        dve.wait_ge(*((s_used, b_last + 1) if n == KT - 1 else (s_down, down + n + 1)))
                    V.scalar_tensor_tensor(out=xT[:, n, :], in0=ps[:, n, :], scalar=scale, in1=xT[:, n, :],
                                           op0=ALU.mult, op1=ALU.add).then_inc(s_x, 1)

            def ffn(p):
                if p.half % 2 == 0:
                    norm(p.norm, p.upd)
                per = 2 * p.step

                def round_(i):
                    for k in range(p.step):
                        if p.swiglu and k == 0:
                            dve.wait_ge(s_used, i * 2 + (p.b + 2))
                        dve.wait_ge(s_sg, i * p.step + (p.tile + k + 1))
                        other = ps[:, 2 + k, :] if p.swiglu else sg[:, k, :]
                        dv.link(V.tensor_tensor(t1[:, k % 2, :], sg[:, k, :], other, ALU.mult))
                        dv.link(V.tensor_scalar(gh[:, ds(i * p.step + k, 1), :], t1[:, k % 2:k % 2 + 1, :], 1.0, None,
                                                ALU.mult))
                        split_lo(gl[:, ds(i * p.step + k, 1), :], t1[:, k % 2:k % 2 + 1, :],
                                 gh[:, ds(i * p.step + k, 1), :], s_g)

                dve.wait_ge(s_hl, 8 * hn(p.norm) + 8)
                with dve.Fori(0, p.iters) as i:
                    dv.enter(i, per)
                    round_(i)
                dv.leave(p.iters)
                update(p.down, p.b + p.up_blocks + p.down_blocks - 1, False, p.scale)

            V.memset(gate_w[:, :, :], 0.0).then_inc(s_vconst, 1)
            V.memset(one[:, :], 1.0).then_inc(s_vconst, 1)
            V.memset(halfpi[:, :], float(np.pi / 2)).then_inc(s_vconst, 1)
            V.memset(small[:, :], 0.0).then_inc(s_vconst, 1)
            V.memset(lam[:, :], 0.0).then_inc(s_vconst, 1)
            for i in range(ROT):
                dv.done(V.memset(rt[:, 3, :, i:i + 1], ROPE_INV[i]))
            dve.wait_ge(s_tr0, 1)
            V.tensor_copy(params[:, :], ps[:, 7, 0:NPARAM]).then_inc(s_par, 1)
            for t in range(KT):
                dve.wait_ge(s_tr0, t + 2)
                V.tensor_copy(xT[:, t, :], ps[:, t, :]).then_inc(s_x, 1)
            dve.wait_ge(s_in2, 16 * (1 + len(ROWP) + 2))
            dve.wait_ge(s_par, 1)
            dv.link(V.tensor_copy(rt[:, 0, :, 0:1], posi[:, :].unsqueeze(2)))
            dv.link(V.tensor_tensor(rt[:, 1, :, :], rt[:, 0, :, 0:1].broadcast_to([P, ST, ROT]), rt[:, 3, :, :],
                                    ALU.mult))
            dv.link(V.tensor_scalar(rt[:, 2, :, :], rt[:, 1, :, :], float(1 / (2 * np.pi)), 12582912.0,
                                    ALU.mult, ALU.add))
            dv.link(V.tensor_scalar(rt[:, 2, :, :], rt[:, 2, :, :], 12582912.0, None, ALU.subtract))
            for part in TWO_PI:
                dv.link(V.scalar_tensor_tensor(out=rt[:, 1, :, :], in0=rt[:, 2, :, :], scalar=-part,
                                               in1=rt[:, 1, :, :], op0=ALU.mult, op1=ALU.add))
            for cut, op in ((float(np.pi), ALU.is_gt), (-float(np.pi), ALU.is_lt)):
                dv.link(V.tensor_scalar(rt[:, 2, :, :], rt[:, 1, :, :], cut, None, op))
                dv.link(V.scalar_tensor_tensor(out=rt[:, 1, :, :], in0=rt[:, 2, :, :],
                                               scalar=float(-2 * np.pi) if cut > 0 else float(2 * np.pi),
                                               in1=rt[:, 1, :, :], op0=ALU.mult, op1=ALU.add))
            PI_IN = float(np.nextafter(np.float32(np.pi), np.float32(0)))
            V.tensor_scalar(rt[:, 0, :, :], rt[:, 1, :, :], PI_IN, -PI_IN, ALU.min, ALU.max).then_inc(s_ang, 1)
            dv.done(V.tensor_scalar(row("diff_q_norm_2"), row("diff_q_norm_2"), -0.125, None, ALU.mult))
            dv.done(V.tensor_scalar(row("dsa_q_norm_2"), row("dsa_q_norm_2"), -0.125, None, ALU.mult))
            dv.done(V.tensor_scalar(row("diff_subln_2"), row("diff_subln_2"), 1.0 - LAM_INIT, None, ALU.mult))
            for c in range(2):
                dv.link(V.tensor_tensor(lam_tmp[:, :], row(f"diff_lam_q{c + 1}_2"), row(f"diff_lam_k{c + 1}_2"),
                                        ALU.mult))
                dv.link(V.tensor_reduce(lam[:, c:c + 1], lam_tmp[:, :], AX_X, ALU.add))
            V.tensor_copy(lam[:, 3:4], lam[:, 0:1]).then_inc(s_lam, 1)

            def mix(b, upd, down):
                norm(N_MIX, upd)
                for k in range(4):
                    d, j = divmod(k, 2)
                    dve.wait_ge(s_mgate, k + 1)
                    V.tensor_scalar(m_g[:, d, j, :], ps[:, (0, 1, 6, 7)[k], :],
                                    col(("gate_fwd_b", "gate_bwd_b")[d], j), None, ALU.add).then_inc(s_mzg, 1)
                dve.wait_ge(s_mlog, 1)
                dv.link(V.scalar_tensor_tensor(out=m_g[:, :, :, :].rearrange("p a b c -> p (a b c)"),
                                               in0=m_g[:, :, :, :].rearrange("p a b c -> p (a b c)"), scalar=0.0,
                                               in1=m_kin[:, :, :, :].rearrange("p a b c -> p (a b c)"),
                                               op0=ALU.min, op1=ALU.subtract))
                for d in range(2):
                    for j in range(2):
                        way = slice(None, None, -1) if d else slice(None)
                        V.tensor_tensor_scan(out=m_b[:, d, j, way], data0=carry[:, :], data1=m_g[:, d, j, way],
                                             initial=0.0, op0=ALU.mult, op1=ALU.add).then_inc(s_mscan, 1)
                dve.wait_ge(s_mscan, 4)
                dve.wait_ge(s_mexp, 2)
                flat = lambda m: m[:, :, :, :].rearrange("p d j c -> p (d j c)")
                q2, k2, r2 = flat(m_qin), flat(m_kin), flat(m_tmp)
                dv.link(V.tensor_tensor(r2, q2, k2, ALU.mult))
                dv.link(V.reciprocal(r2, r2))
                dv.done(V.tensor_tensor(flat(m_kst), q2, r2, ALU.mult))
                dv.link(V.tensor_tensor(r2, k2, r2, ALU.mult))
                dv.done(V.tensor_tensor(q2, flat(m_kst), q2, ALU.mult))
                V.tensor_tensor(k2, r2, k2, ALU.mult).then_inc(s_mhalf, 1)
                dv.wait()
                for d, e in ((0, CH - 1), (1, 0)):
                    V.tensor_copy(m_dech[:, d, :, :], m_qin[:, d, :, e:S:CH]).then_inc(s_mhalf, 1)
                dve.wait_ge(s_mhalf, 3)
                dv.done(V.tensor_tensor(m_dec[:, :, :, :], m_dech[:, :, :, :], m_dech[:, :, :, :], ALU.mult))
                dv.wait()
                dve.wait_ge(s_mqk, 4)
                dve.wait_ge(s_mexp, 4)
                for d in range(2):
                    V.tensor_tensor(m_kin[:, d, :, :], m_kin[:, d, :, :], m_kT[:, :, :], ALU.mult).then_inc(s_mkin, 1)
                dve.wait_ge(s_mkin, 2)
                chunks = lambda m: m[:, :, :, :].rearrange("p d j (n c) -> p (d j n) c", c=CH)
                decay = m_dech[:, :, :, :].rearrange("p d j n -> p (d j n)").unsqueeze(2).broadcast_to([P, 4 * NCH, CH])
                dv.link(V.tensor_tensor(chunks(m_kst), chunks(m_kin), decay, ALU.mult))
                V.tensor_tensor(chunks(m_kst), chunks(m_kst), decay, ALU.mult).then_inc(s_mkin, 1)
                for d in range(2):
                    V.tensor_tensor(m_qin[:, d, :, :], m_qin[:, d, :, :], m_qT[:, :, :], ALU.mult).then_inc(s_mkin, 1)
                dve.wait_ge(s_mkin, 5)
                for k in range(4):
                    dve.wait_ge(s_mkt, k + 1)
                    V.tensor_copy(m_kst_row[:, k // 2, k % 2, :, :].rearrange("p t d -> p (t d)"),
                                  ps[:, (0, 1, 6, 7)[k], :]).then_inc(s_mktc, 1)
                for d in range(2):
                    for step in range(NCH - 1):
                        for j in range(2):
                            if step == 0:
                                dve.wait_ge(s_mds, 2 * d + j + 1)
                            n = NCH - 1 - step if d else step
                            to = n - 1 if d else n + 1
                            src = ps[:, (0, 1, 6, 7)[2 * j + n % 2], ts(n // 2, GDV)]
                            if step == 0:
                                V.tensor_copy(m_state[:, d, j, to, :], src).then_inc(s_mst, 1)
                            else:
                                dve.wait_ge(s_mst, 14 * d + 2 * step + j - 1)
                                V.scalar_tensor_tensor(out=m_state[:, d, j, to, :], in0=m_state[:, d, j, n, :],
                                                       scalar=m_dec[:, d, j, n:n + 1], in1=src, op0=ALU.mult,
                                                       op1=ALU.add).then_inc(s_mst, 1)

                def masked(h):
                    dve.wait_ge(s_matt, h + 1)
                    v4 = m_att[:, h, :].rearrange("p (t c) -> p t c", c=P)
                    tmp = t1[:, 0, :].rearrange("p (t c) -> p t c", c=P)
                    for d, dst in ((0, v4), (1, tmp)):
                        src = ps[:, (0, 1, 6, 7)[2 * (h % 2) + d], :].rearrange("p (t c) -> p t c", c=P)
                        hi_ = cap[:, d:d + 1, :].broadcast_to([P, ST, P])
                        lo_ = ncap[:, d:d + 1, :].broadcast_to([P, ST, P])
                        dv.link(V.tensor_tensor(dst, src, hi_, ALU.min))
                        dv.link(V.tensor_tensor(dst, dst, lo_, ALU.max))
                    V.tensor_tensor(m_att[:, h, :], m_att[:, h, :], t1[:, 0, :], ALU.add).then_inc(s_matc, 1)
                    dve.wait_ge(s_matc, h + 1)

                def gated(j):
                    dve.wait_ge(s_used, b + 9 + j + 1)
                    dve.wait_ge(s_mc, 2 * j + 2)
                    for n in range(2):
                        V.tensor_tensor(m_u[:, 2 * j + n, :], m_u[:, 2 * j + n, :], ps[:, 2 + 2 * j + n, :],
                                        ALU.mult).then_inc(s_mu, 1)

                def convolved(t):
                    w = [col("conv_w", 4 * i + t) for i in range(3)]
                    c, u = m_conv[:, t, :], m_u[:, t, :]
                    dve.wait_ge(s_mu, t + 1)
                    dv.link(V.tensor_scalar(c, u, w[1], col("conv_b", t), ALU.mult, ALU.add))
                    dv.link(V.scalar_tensor_tensor(out=c[:, 1:S], in0=u[:, 0:S - 1], scalar=w[0], in1=c[:, 1:S],
                                                   op0=ALU.mult, op1=ALU.add))
                    dv.link(V.scalar_tensor_tensor(out=c[:, 0:S - 1], in0=u[:, 1:S], scalar=w[2],
                                                   in1=c[:, 0:S - 1], op0=ALU.mult, op1=ALU.add))

                masked(0)
                masked(1)
                gated(0)
                masked(2)
                masked(3)
                convolved(0)
                convolved(1)
                gated(1)
                for h in range(GH):
                    dve.wait_ge(s_mot, h + 1)
                    V.tensor_copy(m_o[:, h, :], ps[:, (0, 1, 6, 7)[h], :]).then_inc(s_mo, 1)
                convolved(2)
                convolved(3)
                dve.wait_ge(s_mr, 4)
                for h in range(GH):
                    dve.wait_ge(s_mo, h + 1)
                    dv.done(V.scalar_tensor_tensor(out=m_r[:, h, :], in0=m_o[:, h, :], scalar=col("gla_norm", h),
                                                   in1=m_r[:, h, :], op0=ALU.mult, op1=ALU.mult))
                for h in range(GH):
                    dve.wait_ge(s_mss, h + 1)
                    half(m_half[:, h, :], ps[:, (0, 1, 6, 7)[h], :], GDV, s_mvar)

                def lo(k):
                    dve.wait_ge(s_mhi, k + 1)
                    src = m_r[:, k, :] if k < GH else m_u[:, k - GH, :]
                    split_lo(m_lo[:, k, :], src, m_hi[:, k, :], s_mfin)

                dv.wait()
                for k in range(KT):
                    if k < GH:
                        dve.wait_ge(s_mrstd, k + 1)
                        refine(m_rstd[:, k, :], m_half[:, k, :], t1[:, k % 2, :])
                        V.tensor_tensor(m_r[:, k, :], m_r[:, k, :], m_rstd[:, k, :], ALU.mult).then_inc(s_mn, 1)
                    else:
                        t = k - GH
                        dve.wait_ge(s_used, b + 11 + t // 2 + 1)
                        V.tensor_tensor(m_u[:, t, :], m_conv[:, t, :], ps[:, 2 + t, :], ALU.mult).then_inc(s_mn, 1)
                    if k:
                        lo(k - 1)
                lo(KT - 1)
                update(down, b + MIX_BLOCKS + OUT_BLOCKS - 1, True)

            def xattn(b, upd, down):
                for t in range(KT):
                    dve.wait_ge(s_xmT, t + 1)
                    V.tensor_copy(x_memT[:, t, :], ps[:, 4 + t % 4, 0:NMEM]).then_inc(s_xm, 1)
                dve.wait_ge(s_xmss, KT)
                half(t1[:, 0, 0:NMEM], ps[:, 0, 0:NMEM], D, s_xmvar)
                dve.wait_ge(s_xmrstd, 1)
                refine(rstd[:, 0:NMEM], t1[:, 0, 0:NMEM], t1[:, 1, 0:NMEM])

                def mlo(t):
                    dve.wait_ge(s_xmh, t + 1)
                    split_lo(x_ml[:, t, :], t1[:, t % 2, 0:NMEM], x_mh[:, t, :], s_xml)

                for t in range(KT):
                    if t >= 2:
                        dve.wait_ge(s_xml, t - 1)
                    V.scalar_tensor_tensor(out=t1[:, t % 2, 0:NMEM], in0=x_memT[:, t, :],
                                           scalar=col("mem_norm", t), in1=rstd[:, 0:NMEM], op0=ALU.mult,
                                           op1=ALU.mult).then_inc(s_xmt1, 1)
                    if t:
                        mlo(t - 1)
                mlo(KT - 1)
                dve.wait_ge(s_xml, 8)
                norm(N_X, upd)

                def max_(h):
                    dve.wait_ge(s_xs, h + 1)
                    banks = ps[:, 2 * (h % 2):2 * (h % 2) + 2, :].rearrange("p b (q m) -> p (b q) m", m=NMEM)
                    dv.link(V.tensor_reduce(small[:, 32 + 4 * h:36 + 4 * h], banks, AX_X, ALU.max))
                    V.tensor_scalar(small[:, 4 * h:4 * h + 4], small[:, 32 + 4 * h:36 + 4 * h], -1.0 / 16.0, None,
                                    ALU.mult).then_inc(s_xmax, 1)

                def normalise(h):
                    dve.wait_ge(s_xe, 4 * h + 4)
                    dv.link(V.reciprocal(small[:, 48 + 4 * h:52 + 4 * h], small[:, 16 + 4 * h:20 + 4 * h]))
                    V.tensor_tensor(x_p[:, h % 2, :, :], x_p[:, h % 2, :, :],
                                    small[:, 48 + 4 * h:52 + 4 * h].unsqueeze(2).broadcast_to([P, ST, NMEM]),
                                    ALU.mult).then_inc(s_xn, 1)

                def parts(h):
                    dve.wait_ge(s_xo, h + 1)
                    if h == 0:
                        dve.wait_ge(s_used, b + X_BLOCKS)
                    for e in range(2):
                        dv.link(V.tensor_copy(hh[:, 2 * h + e, :], ps[:, 6 + e, :]))
                        split_lo(hl[:, 2 * h + e, :], ps[:, 6 + e, :], hh[:, 2 * h + e, :], s_xol)

                max_(0)
                for h in range(4):
                    if h < 3:
                        max_(h + 1)
                    normalise(h)
                    if h:
                        parts(h - 1)
                parts(3)
                update(down, b + X_BLOCKS + OUT_BLOCKS - 1, True)

            def norm_rotate(rows, rs, gain, nh):
                if rs is not None:
                    dv.link(V.tensor_tensor(rows, rows, rs.unsqueeze(3).broadcast_to([P, ST, nh, 64]), ALU.mult))
                if gain is not None:
                    flat = rows.rearrange("p t h d -> p (t h) d")
                    dv.link(V.tensor_tensor(flat, flat, gain.unsqueeze(1).broadcast_to([P, ST * nh, 64]), ALU.mult))
                c = cosr[:, :, :].unsqueeze(2).broadcast_to([P, ST, nh, ROT])
                s = sinr[:, :, :].unsqueeze(2).broadcast_to([P, ST, nh, ROT])
                x1, x2 = rows[:, :, :, 0:ROT], rows[:, :, :, ROT:2 * ROT]
                tmp = [t1[:, 0, i * 256:i * 256 + ST * nh * ROT].rearrange("p (t h r) -> p t h r", t=ST, h=nh)
                       for i in range(2)]
                tmp += [t1[:, 1, i * 256:i * 256 + ST * nh * ROT].rearrange("p (t h r) -> p t h r", t=ST, h=nh)
                        for i in range(2)]
                dv.done(V.tensor_tensor(tmp[0], x1, c, ALU.mult))
                dv.done(V.tensor_tensor(tmp[1], x2, s, ALU.mult))
                dv.done(V.tensor_tensor(tmp[2], x2, c, ALU.mult))
                dv.link(V.tensor_tensor(tmp[3], x1, s, ALU.mult))
                dv.done(V.tensor_tensor(x1, tmp[0], tmp[1], ALU.subtract))
                return V.tensor_tensor(x2, tmp[2], tmp[3], ALU.add)

            def head_sums(dst):
                return V.tensor_reduce(dst, a_sq[:, :, :].rearrange("p t (h d) -> p (t h) d", d=64), AX_X, ALU.add)

            def staged(slot):
                return a_rows[:, slot, :, :].rearrange("p t (h d) -> p t h d", d=64)

            def diff(b, upd, down):
                norm(N_DIFF, upd)
                dve.wait_ge(s_rope, 2)
                dv.wait()
                for g in range(4):
                    dve.wait_ge(s_rcopy, 4 * g + 4)
                    if g:
                        dve.wait_ge(s_rows, g)
                    head_sums(small[:, 32:64]).then_inc(s_rss, 1)
                    dve.wait_ge(s_rss, g + 1)
                    half(newton[:, 0, 0:32], small[:, 32:64], 64, s_rvar)
                    dve.wait_ge(s_rrs, g + 1)
                    refine(small[:, 0:32], newton[:, 0, 0:32], newton[:, 1, 0:32])
                    norm_rotate(staged(g % 2), small[:, 0:32].rearrange("p (t h) -> p t h", t=ST),
                                row("diff_q_norm_2" if g < 2 else "diff_k_norm_2"), 8).then_inc(s_rows, 1)
                dve.wait_ge(s_lam2, 2)
                dv.link(V.tensor_tensor(lam[:, 2:3], lam[:, 1:2], lam[:, 0:1], ALU.subtract))
                dv.link(V.tensor_scalar(lam[:, 2:3], lam[:, 2:3], -LAM_INIT, None, ALU.add))
                dve.wait_ge(s_rows, 4)

                def max_(u):
                    h, qt = divmod(u, 4)
                    nk = P * (qt + 1)
                    dve.wait_ge(s_ds, u + 1)
                    two = ps[:, 2 * (u % 2):2 * (u % 2) + 2, 0:nk]
                    dv.link(V.memset(two[0:CH, :, nk - CH:nk], -NEG))
                    V.tensor_reduce(small[:, 2 * (u % 2):2 * (u % 2) + 2], two, AX_X, ALU.min).then_inc(s_dmax, 1)

                def weights(u):
                    h, qt = divmod(u, 4)
                    nk = P * (qt + 1)
                    dve.wait_ge(s_de, 2 * u + 2)
                    k, r = 4 + 2 * (u % 2), 32 + 8 * (h % 2) + 2 * qt
                    dv.link(V.reciprocal(small[:, r:r + 2], small[:, k:k + 2]))
                    dv.link(V.tensor_scalar(small[:, 8:9], small[:, k:k + 1], small[:, r + 1:r + 2], lam[:, 2:3],
                                            ALU.mult, ALU.mult))
                    if u >= 2:
                        dve.wait_ge(s_dT, u - 1)
                    V.scalar_tensor_tensor(out=d_a[:, u % 2, 0:nk], in0=d_p[:, u % 2, 1, 0:nk],
                                           scalar=small[:, 8:9], in1=d_p[:, u % 2, 0, 0:nk], op0=ALU.mult,
                                           op1=ALU.add).then_inc(s_da, 1)

                def rows_copy(h):
                    dve.wait_ge(s_dpv, 4 * h + 4)
                    if h >= 2:
                        dve.wait_ge(s_doT, h - 1)
                    inv = small[:, 32 + 8 * (h % 2):40 + 8 * (h % 2):2].unsqueeze(2).broadcast_to([P, ST, P])
                    V.tensor_tensor(d_o[:, h % 2, :].rearrange("p (t e) -> p t e", e=P),
                                    ps[:, 6 + h % 2, :].rearrange("p (t e) -> p t e", e=P), inv, ALU.mult)\
                        .then_inc(s_dor, 1)

                def row_sums(h):
                    dve.wait_ge(s_dosq, h + 1)
                    V.tensor_reduce(small[:, 16:20], d_osq[:, :].rearrange("p (t e) -> p t e", e=P), AX_X,
                                    ALU.add).then_inc(s_doss, 1)
                    dve.wait_ge(s_doss, h + 1)
                    half(newton[:, 0, 0:4], small[:, 16:20], P, s_dovar)

                def rows_norm(h):
                    dve.wait_ge(s_dors, h + 1)
                    refine(small[:, 20:24], newton[:, 0, 0:4], newton[:, 1, 0:4])
                    o = d_o[:, h % 2, :].rearrange("p (t e) -> p t e", e=P)
                    dv.link(V.tensor_tensor(o, o, small[:, 20:24].unsqueeze(2).broadcast_to([P, ST, P]), ALU.mult))
                    V.tensor_tensor(o, o, row("diff_subln_2").unsqueeze(1).broadcast_to([P, ST, P]), ALU.mult)\
                        .then_inc(s_don, 1)

                def parts(h):
                    dve.wait_ge(s_doT, h + 1)
                    bank = ps[:, 6 + h % 2, :]
                    dv.link(V.tensor_copy(hh[:, h, :], bank))
                    split_lo(hl[:, h, :], bank, hh[:, h, :], s_dhl)

                dve.wait_ge(s_used, b + DIFF_BLOCKS)
                max_(0)
                max_(1)
                weights(0)
                for u in range(32):
                    h, qt = divmod(u, 4)
                    if u < 31:
                        weights(u + 1)
                    if u < 30:
                        max_(u + 2)
                    if qt == 0 and h >= 2:
                        parts(h - 2)
                    elif qt and h:
                        (rows_copy, row_sums, rows_norm)[qt - 1](h - 1)
                rows_copy(7)
                row_sums(7)
                rows_norm(7)
                parts(6)
                parts(7)
                update(down, b + DIFF_BLOCKS + OUT_BLOCKS - 1, True)

            def dsa(b, upd, down):
                norm(N_DSA, upd)
                dve.wait_ge(s_ccq, ST)
                half(newton[:, 0, 0:4], small[:, 32:36], 256, s_rvar)
                dve.wait_ge(s_ccqr, 1)
                refine(small[:, 36:40], newton[:, 0, 0:4], newton[:, 1, 0:4])
                dve.wait_ge(s_rcopy, 28)
                dv.link(V.tensor_tensor(c_cq[:, :, :], c_cq[:, :, :],
                                        small[:, 36:40].unsqueeze(2).broadcast_to([P, ST, 256]), ALU.mult))
                V.tensor_tensor(c_cq[:, :, :], c_cq[:, :, :],
                                row("dsa_cq_norm_2").unsqueeze(1).broadcast_to([P, ST, 256]), ALU.mult)\
                    .then_inc(s_ccqn, 1)
                dve.wait_ge(s_rcopy, 32)
                dve.wait_ge(s_cid, ST)
                half(newton[:, 0, 0:4], small[:, 40:44], 64, s_rvar)
                dve.wait_ge(s_cidr, 1)
                refine(small[:, 44:48], newton[:, 0, 0:4], newton[:, 1, 0:4])
                kid = c_kid[:, :, 0:64].unsqueeze(2)
                dv.link(norm_rotate(kid, small[:, 44:48].unsqueeze(2), None, 1))
                V.tensor_copy(c_kid[:, :, 64:128], c_kid[:, :, 0:64]).then_inc(s_cidn, 1)
                for k in range(2):
                    dve.wait_ge(s_cqT, k + 1)
                    dve.wait_ge(s_cqh, k + 1)
                    split_lo(c_cql[:, k, :], ps[:, 4 + k, :], c_cqh[:, k, :], s_cql)

                def finish(g, slot, gain, rcopy):
                    dve.wait_ge(s_rcopy, rcopy)
                    head_sums(c_rs[:, 32:64]).then_inc(s_rss2, 1)
                    dve.wait_ge(s_rss2, g + 1)
                    half(newton[:, 0, 0:32], c_rs[:, 32:64], 64, s_rvar)
                    dve.wait_ge(s_rrs2, g + 1)
                    refine(c_rs[:, 0:32], newton[:, 0, 0:32], newton[:, 1, 0:32])
                    norm_rotate(staged(slot), c_rs[:, 0:32].rearrange("p (t h) -> p t h", t=ST), row(gain), 8)\
                        .then_inc(s_rows, 1)
                    dve.wait_ge(s_rows, (5, 7, 8, 9)[g])

                finish(0, 0, "dsa_k_norm_2", 36)
                dve.wait_ge(s_rcopy, 40)
                norm_rotate(staged(1), None, None, 8).then_inc(s_rows, 1)
                dve.wait_ge(s_rows, 6)
                off = [0, 128, 384, 768]
                for v in range(32):
                    qt, h = divmod(v, IH)
                    nk = P * (qt + 1)
                    dve.wait_ge(s_crelu, v + 1)
                    w = small[:, 8 * qt + h:8 * qt + h + 1]
                    sc = c_score[:, off[qt]:off[qt] + nk]
                    if h == 0:
                        V.tensor_scalar(sc, c_relu[:, v % 2, 0:nk], w, None, ALU.mult).then_inc(s_cacc, 1)
                    else:
                        dve.wait_ge(s_cacc, v)
                        V.scalar_tensor_tensor(out=sc, in0=c_relu[:, v % 2, 0:nk], scalar=w, in1=sc,
                                               op0=ALU.mult, op1=ALU.add).then_inc(s_cacc, 1)
                dve.wait_ge(s_cacc, 32)
                dv.done(V.memset(c_bias[:, 0:P], 0.0))
                for qt in range(1, ST):
                    e = off[qt] + P * (qt + 1)
                    dv.done(V.memset(c_score[0:CH, e - CH:e], NEG))
                dv.wait()
                dv.link(V.memset(c_bias[0:CH, P - CH:P], -NEG))

                def top(qt):
                    c = slice(off[qt], off[qt] + P * (qt + 1))
                    for r in range(TOPK // 8):
                        src = c_work if r else c_score
                        dv.link(V.max(c_best[:, :], src[:, c]))
                        dv.link(V.match_replace(out=c_work[:, c], in_to_replace=c_best[:, :], in_values=src[:, c],
                                                imm_value=GONE))
                    dv.link(V.tensor_tensor(c_bias[:, c], c_work[:, c], c_score[:, c], ALU.is_equal))
                    dv.link(V.tensor_scalar(c_bias[:, c], c_bias[:, c], -NEG, None, ALU.mult))

                finish(1, 0, "dsa_q_norm_2", 44)
                finish(2, 1, "dsa_q_norm_2", 48)
                top(1)
                finish(3, 0, "dsa_k_norm_2", 52)
                top(2)
                top(3)
                dve.wait_ge(s_used, b + DSA_BLOCKS)
                dve.wait_ge(s_rt, 36)

                def mask_max(u):
                    h, qt = divmod(u, 4)
                    nk = P * (qt + 1)
                    dve.wait_ge(s_cs0, u + 1)
                    if u >= 4:
                        dve.wait_ge(s_ce, u - 3)
                    V.tensor_tensor_reduce(out=c_s[:, u % 4, 0:nk], in0=ps[:, u % 4, 0:nk],
                                           in1=c_bias[:, off[qt]:off[qt] + nk], scale=1.0, scalar=3.0e38,
                                           op0=ALU.add, op1=ALU.min,
                                           accum_out=small[:, u % 4:u % 4 + 1]).then_inc(s_cs, 1)

                def half_copy(u):
                    nk = P * (u % 4 + 1)
                    dve.wait_ge(s_cT, u + 1)
                    if u >= 2:
                        dve.wait_ge(s_cpv, u - 1)
                    V.tensor_copy(c_pT[:, u % 2, 0:nk], ps[:, 4 + u % 2, 0:nk]).then_inc(s_cpTd, 1)

                def rows_out(j):
                    dve.wait_ge(s_cpv, 8 * j + 8)
                    k = 16 + 8 * (j % 2)
                    dv.link(V.reciprocal(small[:, 32:40], small[:, k:k + 8]))
                    if j >= 2:
                        dve.wait_ge(s_coT, j - 1)
                    inv = small[:, 32:40].rearrange("p (a t) -> p t a", a=2).unsqueeze(3)
                    V.tensor_tensor(c_o[:, j % 2, :].rearrange("p (t a e) -> p t a e", t=ST, a=2),
                                    ps[:, 6 + j % 2, :].rearrange("p (t a e) -> p t a e", t=ST, a=2),
                                    inv.broadcast_to([P, ST, 2, 64]), ALU.mult).then_inc(s_cor, 1)
                    dve.wait_ge(s_cor, j + 1)

                def parts(j):
                    dve.wait_ge(s_coT, j + 1)
                    bank = ps[:, 6 + j % 2, :]
                    dv.link(V.tensor_copy(hh[:, j, :], bank))
                    split_lo(hl[:, j, :], bank, hh[:, j, :], s_chl)

                for u in range(3):
                    mask_max(u)
                for u in range(64):
                    if u and u % 2 == 0:
                        half_copy(u - 1)
                    if u < 61:
                        mask_max(u + 3)
                    if u % 8 == 1 and u > 8:
                        rows_out(u // 8 - 1)
                    if u % 8 == 4 and u > 8:
                        parts(u // 8 - 1)
                half_copy(63)
                rows_out(7)
                parts(7)
                update(down, b + DSA_BLOCKS + OUT_BLOCKS - 1, True)

            for stage in stages:
                if isinstance(stage, Pass):
                    ffn(stage)
                elif stage == "final":
                    norm(N_FINAL, at["final"][1])
                else:
                    {"mix": mix, "x": xattn, "diff": diff, "dsa": dsa}[stage[0]](*at[stage[0]])
            for k in range(0, 2 * ST, 2):
                dve.wait_ge(s_ot, k + 1)
                V.tensor_copy(orows[:, k // 2, 0:512], ps[:, k, :]).then_inc(s_orow_v, 1)


_OUT = "out_0_dram"


def kernel(**inputs):
    import concourse.bacc as bacc
    from concourse.bass_utils import run_bass_kernel_spmd

    nc = bacc.Bacc("TRN2", target_bir_lowering=False, num_devices=1, dynamic_dma_scratch_size=1024)
    arrays, dram = {}, {}
    for name in inputs:
        a = np.ascontiguousarray(inputs[name])
        arrays["in_" + name] = a
        dram[name] = nc.dram_tensor("in_" + name, a.shape, mybir.dt.from_np(a.dtype), kind="ExternalInput").ap()
    out = nc.dram_tensor(_OUT, (1, S, D), F32, kind="ExternalOutput").ap()
    two_blocks(nc, dram, out)
    return run_bass_kernel_spmd(nc, [arrays], core_ids=[0]).results[0][_OUT]
```
